# Optimizing a Trainium2 kernel written in Bass

```python
import math
import jax, jax.numpy as jnp
from jax import lax
import numpy as np

D_MODEL = 1024
BATCH = 1
SEQ = 512
DEPTH = 1

MIX_WIDTH = D_MODEL
NSA_WIDTH = MIX_WIDTH // 2
NSA_HEAD_DIM = 64
NSA_HEADS = NSA_WIDTH // NSA_HEAD_DIM
NSA_KV_HEADS = 2
NSA_GROUP = NSA_HEADS // NSA_KV_HEADS
NSA_KV_WIDTH = NSA_KV_HEADS * NSA_HEAD_DIM
CMP_STRIDE = 16
CMP_BLOCK = 2 * CMP_STRIDE
CMP_HIDDEN = 4 * NSA_HEAD_DIM
SEL_BLOCK = 64
N_SELECT = 16
WINDOW = 512
Q_BLOCK = 128
FORCED_SCORE = 1.0e4
MLSTM_WIDTH = MIX_WIDTH - NSA_WIDTH
MLSTM_HEADS = 4
MLSTM_V_DIM = MLSTM_WIDTH // MLSTM_HEADS
MLSTM_QK_DIM = MLSTM_V_DIM // 2
MLSTM_QK_WIDTH = MLSTM_HEADS * MLSTM_QK_DIM
MLSTM_CHUNK = 64
CONV_WIDTH = 4
REL_BUCKETS = 32
REL_MAX_DISTANCE = 128
MEM_TOKENS = 256
XATTN_HEADS = 4
XATTN_HEAD_DIM = D_MODEL // XATTN_HEADS
D_FF = -(-8 * D_MODEL // (3 * 256)) * 256
NORM_EPS = 1e-6
NEG_INF = -1.0e30

IN_SIZES = (NSA_WIDTH,) + (NSA_KV_WIDTH,) * 6 + (NSA_HEADS * 3, MLSTM_QK_WIDTH, MLSTM_QK_WIDTH,
            MLSTM_WIDTH, MLSTM_HEADS, MLSTM_HEADS, MLSTM_WIDTH)
IN_WIDTH = sum(IN_SIZES)
IN_OFFSETS = tuple(int(o) for o in np.cumsum(IN_SIZES)[:-1])


def rms_norm(x, gain):
    xf = x.astype(jnp.float32)
    y = xf * lax.rsqrt(jnp.mean(xf * xf, axis=-1, keepdims=True) + NORM_EPS)
    return (y * gain.astype(jnp.float32)).astype(x.dtype)

def rel_bucket(dist):
    n = jnp.maximum(dist, 0)
    max_exact = REL_BUCKETS // 2
    nf = jnp.maximum(n, 1).astype(jnp.float32)
    large = max_exact + (jnp.log(nf / max_exact) / math.log(REL_MAX_DISTANCE / max_exact)
                         * (REL_BUCKETS - max_exact)).astype(jnp.int32)
    large = jnp.minimum(large, REL_BUCKETS - 1)
    return jnp.where(n < max_exact, n, large)

def masked_softmax(s, mask):
    s = jnp.where(mask, s.astype(jnp.float32), NEG_INF)
    return jnp.where(mask, jax.nn.softmax(s, axis=-1), 0.0)

def compress_blocks(kv, pos, w1, w2):
    B, H, S, DH = kv.shape
    c = kv.reshape(B, H, S // CMP_STRIDE, CMP_STRIDE, DH)
    blocks = jnp.concatenate([c[:, :, :-1], c[:, :, 1:]], axis=3) + pos
    hid = jax.nn.silu(blocks.reshape(B, H, -1, CMP_BLOCK * DH) @ w1)
    return hid @ w2

def native_sparse_attention(q, k_cmp, v_cmp, k_slc, v_slc, k_win, v_win, gates, rel_bias):
    B, HKV, G, S, DH = q.shape
    n_cmp = k_cmp.shape[2]
    n_sel = S // SEL_BLOCK
    n_top = min(N_SELECT, n_sel)
    n_kwin = Q_BLOCK + WINDOW
    cmp_start = jnp.arange(n_cmp) * CMP_STRIDE
    cmp_end = cmp_start + (CMP_BLOCK - 1)
    sel_start = jnp.arange(n_sel) * SEL_BLOCK
    overlap = ((cmp_start[:, None] <= sel_start[None, :] + SEL_BLOCK - 1)
               & (cmp_end[:, None] >= sel_start[None, :])).astype(jnp.float32)
    k_blk = k_slc.reshape(B, HKV, n_sel, SEL_BLOCK, DH)
    v_blk = v_slc.reshape(B, HKV, n_sel, SEL_BLOCK, DH)
    k_pad = jnp.pad(k_win, ((0, 0), (0, 0), (WINDOW, 0), (0, 0)))
    v_pad = jnp.pad(v_win, ((0, 0), (0, 0), (WINDOW, 0), (0, 0)))
    gather = jax.vmap(jax.vmap(lambda blocks, idx: blocks[idx]))
    head_off = (jnp.arange(NSA_HEADS) * REL_BUCKETS).reshape(HKV, G)
    bias_flat = rel_bias.reshape(-1)
    blk_ids = jnp.arange(n_sel)

    def head_bias(dist):
        return rel_bias[:, rel_bucket(dist)].reshape(HKV, G, *dist.shape)

    def query_block(c):
        t0 = c * Q_BLOCK
        tq = t0 + jnp.arange(Q_BLOCK)
        qc = lax.dynamic_slice_in_dim(q, t0, Q_BLOCK, axis=3)
        gc = lax.dynamic_slice_in_dim(gates, t0, Q_BLOCK, axis=3)
        d_c = tq[:, None] - cmp_end[None, :]
        s_c = jnp.einsum('bhgtd,bhcd->bhgtc', qc, k_cmp).astype(jnp.float32) + head_bias(d_c)
        p_c = masked_softmax(s_c, d_c >= 0)
        o_c = jnp.einsum('bhgtc,bhcd->bhgtd', p_c.astype(v_cmp.dtype), v_cmp)
        imp = jnp.einsum('bhgtc,cj->bhtj', p_c, overlap)
        cur = tq // SEL_BLOCK
        forced = ((blk_ids[None, :] == 0) | (blk_ids[None, :] == cur[:, None])
                  | (blk_ids[None, :] == cur[:, None] - 1))
        score = jnp.where(forced, FORCED_SCORE, jnp.where(blk_ids[None, :] <= cur[:, None], imp, -1.0))
        _, idx = lax.top_k(score, n_top)
        k_s = gather(k_blk, idx).reshape(B, HKV, Q_BLOCK, n_top * SEL_BLOCK, DH)
        v_s = gather(v_blk, idx).reshape(B, HKV, Q_BLOCK, n_top * SEL_BLOCK, DH)
        kpos = (idx[..., None] * SEL_BLOCK + jnp.arange(SEL_BLOCK)).reshape(B, HKV, Q_BLOCK, n_top * SEL_BLOCK)
        d_s = tq[:, None] - kpos
        b_s = bias_flat[head_off[None, :, :, None, None] + rel_bucket(d_s)[:, :, None]]
        s_s = jnp.einsum('bhgtd,bhtkd->bhgtk', qc, k_s).astype(jnp.float32) + b_s
        p_s = masked_softmax(s_s, (d_s >= 0)[:, :, None])
        o_s = jnp.einsum('bhgtk,bhtkd->bhgtd', p_s.astype(v_s.dtype), v_s)
        k_w = lax.dynamic_slice_in_dim(k_pad, t0, n_kwin, axis=2)
        v_w = lax.dynamic_slice_in_dim(v_pad, t0, n_kwin, axis=2)
        kpos_w = t0 - WINDOW + jnp.arange(n_kwin)
        d_w = tq[:, None] - kpos_w[None, :]
        m_w = (d_w >= 0) & (d_w < WINDOW) & (kpos_w[None, :] >= 0)
        s_w = jnp.einsum('bhgtd,bhkd->bhgtk', qc, k_w).astype(jnp.float32) + head_bias(d_w)
        p_w = masked_softmax(s_w, m_w)
        o_w = jnp.einsum('bhgtk,bhkd->bhgtd', p_w.astype(v_w.dtype), v_w)
        return gc[..., 0:1] * o_c + gc[..., 1:2] * o_s + gc[..., 2:3] * o_w

    return lax.map(query_block, jnp.arange(S // Q_BLOCK))

def causal_depthwise_conv(u, w, b):
    y = lax.conv_general_dilated(u, w[:, None, :].astype(u.dtype), window_strides=(1,),
                                 padding=((CONV_WIDTH - 1, 0),), dimension_numbers=('NWC', 'WIO', 'NWC'),
                                 feature_group_count=u.shape[-1])
    return y + b

def mlstm_chunkwise(q, k, v, i_pre, log_f):
    B, S, H, DK = q.shape
    DV = v.shape[-1]
    L = MLSTM_CHUNK
    nc = S // L
    f32 = jnp.float32

    def chunks(t):
        return t.astype(f32).reshape(B, nc, L, H, -1).transpose(1, 0, 3, 2, 4)

    qs, ks, vs = chunks(q), chunks(k) * (DK ** -0.5), chunks(v)
    ig = chunks(i_pre[..., None])[..., 0]
    lf = chunks(log_f[..., None])[..., 0]
    causal = jnp.tril(jnp.ones((L, L), dtype=bool))

    def step(carry, inp):
        C, n, m = carry
        qc, kc, vc, ic, fc = inp
        b = jnp.cumsum(fc, axis=-1)
        D = jnp.where(causal, b[..., :, None] - b[..., None, :] + ic[..., None, :], NEG_INF)
        m_inter = b + m[..., None]
        m_t = jnp.maximum(m_inter, jnp.max(D, axis=-1))
        w = jnp.exp(D - m_t[..., None])
        a = jnp.exp(m_inter - m_t)
        s = jnp.einsum('bhtd,bhsd->bhts', qc, kc) * w
        num = jnp.einsum('bhts,bhsv->bhtv', s, vc) + a[..., None] * jnp.einsum('bhtd,bhdv->bhtv', qc, C)
        den = jnp.sum(s, axis=-1) + a * jnp.einsum('bhtd,bhd->bht', qc, n)
        h = num / jnp.maximum(jnp.abs(den), jnp.exp(-m_t))[..., None]
        bL = b[..., -1]
        ws = bL[..., None] - b + ic
        m_next = jnp.maximum(bL + m, jnp.max(ws, axis=-1))
        decay = jnp.exp(bL + m - m_next)
        kw = kc * jnp.exp(ws - m_next[..., None])[..., None]
        C = decay[..., None, None] * C + jnp.einsum('bhsd,bhsv->bhdv', kw, vc)
        n = decay[..., None] * n + jnp.sum(kw, axis=2)
        return (C, n, m_next), h

    init = (jnp.zeros((B, H, DK, DV), f32), jnp.zeros((B, H, DK), f32), jnp.zeros((B, H), f32))
    _, hs = lax.scan(step, init, (qs, ks, vs, ig, lf))
    return hs.transpose(1, 0, 3, 2, 4).reshape(B, S, H, DV)

def hybrid_mixer(h, rel_bias, w_in, cmp_pos_k, cmp_pos_v, cmp_w1_k, cmp_w2_k, cmp_w1_v, cmp_w2_v,
                 conv_w, conv_b, mlstm_gate_bias, mlstm_norm, w_out):
    B, S, _ = h.shape
    (nq, kc, vc, ksl, vsl, kwn, vwn, gt, mq, mk, mv, mi, mf, mo) = jnp.split(h @ w_in, IN_OFFSETS, axis=-1)

    def kv_heads(t):
        return t.reshape(B, S, NSA_KV_HEADS, NSA_HEAD_DIM).transpose(0, 2, 1, 3)

    q = nq.reshape(B, S, NSA_KV_HEADS, NSA_GROUP, NSA_HEAD_DIM).transpose(0, 2, 3, 1, 4) * (NSA_HEAD_DIM ** -0.5)
    k_cmp = compress_blocks(kv_heads(kc), cmp_pos_k, cmp_w1_k, cmp_w2_k)
    v_cmp = compress_blocks(kv_heads(vc), cmp_pos_v, cmp_w1_v, cmp_w2_v)
    gates = jax.nn.sigmoid(gt.reshape(B, S, NSA_KV_HEADS, NSA_GROUP, 3).transpose(0, 2, 3, 1, 4))
    o = native_sparse_attention(q, k_cmp, v_cmp, kv_heads(ksl), kv_heads(vsl), kv_heads(kwn), kv_heads(vwn),
                                gates, rel_bias)
    y_nsa = o.transpose(1, 0, 4, 2, 3, 5).reshape(B, S, NSA_WIDTH)

    qk = jax.nn.silu(causal_depthwise_conv(jnp.concatenate([mq, mk], axis=-1), conv_w, conv_b))
    mq, mk = jnp.split(qk, 2, axis=-1)
    hm = mlstm_chunkwise(mq.reshape(B, S, MLSTM_HEADS, MLSTM_QK_DIM), mk.reshape(B, S, MLSTM_HEADS, MLSTM_QK_DIM),
                         mv.reshape(B, S, MLSTM_HEADS, MLSTM_V_DIM),
                         mi.astype(jnp.float32) + mlstm_gate_bias[0].astype(jnp.float32),
                         jax.nn.log_sigmoid(mf.astype(jnp.float32) + mlstm_gate_bias[1].astype(jnp.float32)))
    hm = hm * lax.rsqrt(jnp.mean(hm * hm, axis=-1, keepdims=True) + NORM_EPS)
    hm = (hm.reshape(B, S, MLSTM_WIDTH) * mlstm_norm.astype(jnp.float32)).astype(h.dtype)
    y_ml = jax.nn.sigmoid(mo) * hm

    return jnp.concatenate([y_nsa, y_ml], axis=-1) @ w_out

def memory_cross_attention(h, mem_n, w_xq, w_xkv, w_xo):
    B, S, _ = h.shape
    M = mem_n.shape[1]
    q = (h @ w_xq).reshape(B, S, XATTN_HEADS, XATTN_HEAD_DIM) * (XATTN_HEAD_DIM ** -0.5)
    k, v = jnp.split(mem_n @ w_xkv, 2, axis=-1)
    k = k.reshape(B, M, XATTN_HEADS, XATTN_HEAD_DIM)
    v = v.reshape(B, M, XATTN_HEADS, XATTN_HEAD_DIM)
    p = jax.nn.softmax(jnp.einsum('bshd,bmhd->bhsm', q, k).astype(jnp.float32), axis=-1)
    o = jnp.einsum('bhsm,bmhd->bshd', p.astype(v.dtype), v).reshape(B, S, D_MODEL)
    return o @ w_xo

def swiglu_ffn(h, w_gate_up, w_down):
    g, u = jnp.split(h @ w_gate_up, 2, axis=-1)
    return (jax.nn.silu(g) * u) @ w_down

def first_inputs(seed: int = 0) -> dict:
    key = jax.random.key(seed)
    keys = iter(jax.random.split(key, 40))

    def nrm(shape, scale):
        return scale * jax.random.normal(next(keys), shape, jnp.float32)

    def gain(width=D_MODEL):
        return 1.0 + nrm((DEPTH, width), 0.02)

    inputs = {}
    inputs['x'] = nrm((BATCH, SEQ, D_MODEL), 1.0)
    inputs['mem'] = nrm((BATCH, MEM_TOKENS, D_MODEL), 1.0)
    inputs['rel_bias'] = nrm((NSA_HEADS, REL_BUCKETS), 0.5)
    inputs['mix_norm_pre'] = gain()
    inputs['w_in'] = nrm((DEPTH, D_MODEL, IN_WIDTH), D_MODEL ** -0.5)
    inputs['cmp_pos_k'] = nrm((DEPTH, CMP_BLOCK, NSA_HEAD_DIM), 0.02)
    inputs['cmp_pos_v'] = nrm((DEPTH, CMP_BLOCK, NSA_HEAD_DIM), 0.02)
    inputs['cmp_w1_k'] = nrm((DEPTH, CMP_BLOCK * NSA_HEAD_DIM, CMP_HIDDEN), (CMP_BLOCK * NSA_HEAD_DIM) ** -0.5)
    inputs['cmp_w2_k'] = nrm((DEPTH, CMP_HIDDEN, NSA_HEAD_DIM), CMP_HIDDEN ** -0.5)
    inputs['cmp_w1_v'] = nrm((DEPTH, CMP_BLOCK * NSA_HEAD_DIM, CMP_HIDDEN), (CMP_BLOCK * NSA_HEAD_DIM) ** -0.5)
    inputs['cmp_w2_v'] = nrm((DEPTH, CMP_HIDDEN, NSA_HEAD_DIM), CMP_HIDDEN ** -0.5)
    inputs['conv_w'] = nrm((DEPTH, CONV_WIDTH, 2 * MLSTM_QK_WIDTH), CONV_WIDTH ** -0.5)
    inputs['conv_b'] = nrm((DEPTH, 2 * MLSTM_QK_WIDTH), 0.01)
    forget_bias = jnp.broadcast_to(jnp.linspace(3.0, 6.0, MLSTM_HEADS), (DEPTH, MLSTM_HEADS))
    inputs['mlstm_gate_bias'] = jnp.stack([nrm((DEPTH, MLSTM_HEADS), 0.1),
                                           forget_bias + nrm((DEPTH, MLSTM_HEADS), 0.1)], axis=1)
    inputs['mlstm_norm'] = gain(MLSTM_WIDTH)
    inputs['w_out'] = nrm((DEPTH, MIX_WIDTH, D_MODEL), MIX_WIDTH ** -0.5)
    inputs['mix_norm_post'] = gain()
    inputs['xattn_norm_pre'] = gain()
    inputs['mem_norm'] = gain()
    inputs['w_xq'] = nrm((DEPTH, D_MODEL, D_MODEL), D_MODEL ** -0.5)
    inputs['w_xkv'] = nrm((DEPTH, D_MODEL, 2 * D_MODEL), D_MODEL ** -0.5)
    inputs['w_xo'] = nrm((DEPTH, D_MODEL, D_MODEL), D_MODEL ** -0.5)
    inputs['xattn_norm_post'] = gain()
    inputs['ffn_norm_pre'] = gain()
    inputs['w_gate_up'] = nrm((DEPTH, D_MODEL, 2 * D_FF), D_MODEL ** -0.5)
    inputs['w_down'] = nrm((DEPTH, D_FF, D_MODEL), D_FF ** -0.5)
    inputs['ffn_norm_post'] = gain()
    return inputs

def first_block(x, mem, rel_bias, mix_norm_pre, w_in, cmp_pos_k, cmp_pos_v, cmp_w1_k, cmp_w2_k, cmp_w1_v,
              cmp_w2_v, conv_w, conv_b, mlstm_gate_bias, mlstm_norm, w_out, mix_norm_post, xattn_norm_pre,
              mem_norm, w_xq, w_xkv, w_xo, xattn_norm_post, ffn_norm_pre, w_gate_up, w_down, ffn_norm_post):
    for l in range(DEPTH):
        h = rms_norm(x, mix_norm_pre[l])
        y = hybrid_mixer(h, rel_bias, w_in[l], cmp_pos_k[l], cmp_pos_v[l], cmp_w1_k[l], cmp_w2_k[l],
                         cmp_w1_v[l], cmp_w2_v[l], conv_w[l], conv_b[l], mlstm_gate_bias[l], mlstm_norm[l], w_out[l])
        x = x + rms_norm(y, mix_norm_post[l])
        h = rms_norm(x, xattn_norm_pre[l])
        y = memory_cross_attention(h, rms_norm(mem, mem_norm[l]), w_xq[l], w_xkv[l], w_xo[l])
        x = x + rms_norm(y, xattn_norm_post[l])
        h = rms_norm(x, ffn_norm_pre[l])
        y = swiglu_ffn(h, w_gate_up[l], w_down[l])
        x = x + rms_norm(y, ffn_norm_post[l])
    return x


DEPTH_2 = 2

N_A = DEPTH_2 // 2
N_B = DEPTH_2 - N_A
N_HEADS = 16
HEAD_DIM = D_MODEL // N_HEADS
D_FF_2 = 2816
CONV_WIDTH_2 = 31
RMS_EPS = 1e-6
LN_EPS = 1e-5
HALF_STEP = 0.5


def rms_norm_2(x, g):
    xf = x.astype(jnp.float32)
    y = xf * lax.rsqrt(jnp.mean(xf * xf, axis=-1, keepdims=True) + RMS_EPS)
    return (y * g.astype(jnp.float32)).astype(x.dtype)

def layer_norm(x, g, b):
    xf = x.astype(jnp.float32)
    mu = jnp.mean(xf, axis=-1, keepdims=True)
    xc = xf - mu
    var = jnp.mean(xc * xc, axis=-1, keepdims=True)
    y = xc * lax.rsqrt(var + LN_EPS) * g.astype(jnp.float32) + b.astype(jnp.float32)
    return y.astype(x.dtype)

def swiglu_ffn_2(x, w_gate, w_up, w_down):
    return (jax.nn.silu(x @ w_gate) * (x @ w_up)) @ w_down

def conformer_conv(x, w_pw1, b_pw1, w_dw, b_dw, ln_g, ln_b, w_pw2, b_pw2):
    h = x @ w_pw1 + b_pw1
    a, gate = jnp.split(h, 2, axis=-1)
    h = a * jax.nn.sigmoid(gate)
    h = lax.conv_general_dilated(
        h, w_dw[:, None, :].astype(h.dtype),
        window_strides=(1,), padding=[(CONV_WIDTH_2 - 1, 0)],
        dimension_numbers=('NWC', 'WIO', 'NWC'),
        feature_group_count=D_MODEL) + b_dw
    h = jax.nn.silu(layer_norm(h, ln_g, ln_b))
    return h @ w_pw2 + b_pw2

def split_heads(t):
    b, s, _ = t.shape
    return t.reshape(b, s, N_HEADS, HEAD_DIM).transpose(0, 2, 1, 3)

def stick_breaking_attention(q, k, v):
    s_len = q.shape[2]
    scale = HEAD_DIM ** -0.5
    outs = []
    for blk in range(s_len // Q_BLOCK):
        start = blk * Q_BLOCK
        end = start + Q_BLOCK
        qb = q[:, :, start:end]
        kb = k[:, :, :end]
        vb = v[:, :, :end]
        z = jnp.einsum('bhqd,bhkd->bhqk', qb, kb, preferred_element_type=jnp.float32) * scale
        t_pos = jnp.arange(start, end)[:, None]
        s_pos = jnp.arange(end)[None, :]
        causal = s_pos < t_pos
        log_beta = jax.nn.log_sigmoid(z)
        log_one_minus = jnp.where(causal, jax.nn.log_sigmoid(-z), 0.0)
        log_remain = lax.cumsum(log_one_minus, axis=3, reverse=True) - log_one_minus
        weights = jnp.where(causal, jnp.exp(log_beta + log_remain), 0.0)
        outs.append(jnp.einsum('bhqk,bhkd->bhqd', weights.astype(vb.dtype), vb))
    return jnp.concatenate(outs, axis=2)

def second_inputs(seed: int = 0) -> dict:
    key = jax.random.key(seed)
    ks = jax.random.split(key, 32)
    f32 = jnp.float32

    def w(k, shape, fan_in):
        return jax.random.normal(k, shape, f32) * (fan_in ** -0.5)

    def gain(k, shape):
        return 1.0 + 0.02 * jax.random.normal(k, shape, f32)

    def bias(k, shape):
        return 0.01 * jax.random.normal(k, shape, f32)

    D, F = D_MODEL, D_FF_2
    return {
        "x": jax.random.normal(ks[0], (BATCH, SEQ, D), f32),
        "ffn1_norm": gain(ks[1], (DEPTH_2, D)),
        "ffn1_w_gate": w(ks[2], (DEPTH_2, D, F), D),
        "ffn1_w_up": w(ks[3], (DEPTH_2, D, F), D),
        "ffn1_w_down": w(ks[4], (DEPTH_2, F, D), F),
        "mix_norm": gain(ks[5], (DEPTH_2, D)),
        "ffn2_norm": gain(ks[6], (DEPTH_2, D)),
        "ffn2_w_gate": w(ks[7], (DEPTH_2, D, F), D),
        "ffn2_w_up": w(ks[8], (DEPTH_2, D, F), D),
        "ffn2_w_down": w(ks[9], (DEPTH_2, F, D), F),
        "conv_w_pw1": w(ks[10], (N_A, D, 2 * D), D),
        "conv_b_pw1": bias(ks[11], (N_A, 2 * D)),
        "conv_w_dw": w(ks[12], (N_A, CONV_WIDTH_2, D), CONV_WIDTH_2),
        "conv_b_dw": bias(ks[13], (N_A, D)),
        "conv_ln_g": gain(ks[14], (N_A, D)),
        "conv_ln_b": bias(ks[15], (N_A, D)),
        "conv_w_pw2": w(ks[16], (N_A, D, D), D),
        "conv_b_pw2": bias(ks[17], (N_A, D)),
        "kv_norm": gain(ks[18], (D,)),
        "w_kv": w(ks[19], (D, 2 * D), D),
        "attn_w_q": w(ks[20], (N_B, D, D), D),
        "attn_w_o": w(ks[21], (N_B, D, D), D),
        "final_norm": gain(ks[22], (D,)),
    }

def second_block(x, ffn1_norm, ffn1_w_gate, ffn1_w_up, ffn1_w_down, mix_norm,
              ffn2_norm, ffn2_w_gate, ffn2_w_up, ffn2_w_down,
              conv_w_pw1, conv_b_pw1, conv_w_dw, conv_b_dw, conv_ln_g, conv_ln_b,
              conv_w_pw2, conv_b_pw2, kv_norm, w_kv, attn_w_q, attn_w_o, final_norm):
    b, s, d = x.shape
    h = x
    k_shared = None
    v_shared = None
    for layer in range(DEPTH_2):
        h = h + HALF_STEP * swiglu_ffn_2(rms_norm_2(h, ffn1_norm[layer]),
                                       ffn1_w_gate[layer], ffn1_w_up[layer], ffn1_w_down[layer])
        u = rms_norm_2(h, mix_norm[layer])
        if layer < N_A:
            i = layer
            h = h + conformer_conv(u, conv_w_pw1[i], conv_b_pw1[i], conv_w_dw[i], conv_b_dw[i],
                                   conv_ln_g[i], conv_ln_b[i], conv_w_pw2[i], conv_b_pw2[i])
        else:
            i = layer - N_A
            q = split_heads(u @ attn_w_q[i])
            o = stick_breaking_attention(q, k_shared, v_shared)
            o = o.transpose(0, 2, 1, 3).reshape(b, s, d)
            h = h + o @ attn_w_o[i]
        h = h + HALF_STEP * swiglu_ffn_2(rms_norm_2(h, ffn2_norm[layer]),
                                       ffn2_w_gate[layer], ffn2_w_up[layer], ffn2_w_down[layer])
        if layer == N_A - 1:
            kv = rms_norm_2(h, kv_norm) @ w_kv
            k_flat, v_flat = jnp.split(kv, 2, axis=-1)
            k_shared = split_heads(k_flat)
            v_shared = split_heads(v_flat)
    return rms_norm_2(h, final_norm)


def setup_inputs(seed=0):
    out = dict(first_inputs(seed))
    for name, value in second_inputs(seed + 1).items():
        if name != "x":
            out[name + "_2"] = value
    return out


def reference(
    x, mem, rel_bias, mix_norm_pre, w_in, cmp_pos_k, cmp_pos_v, cmp_w1_k, cmp_w2_k, cmp_w1_v,
    cmp_w2_v, conv_w, conv_b, mlstm_gate_bias, mlstm_norm, w_out, mix_norm_post, xattn_norm_pre,
    mem_norm, w_xq, w_xkv, w_xo, xattn_norm_post, ffn_norm_pre, w_gate_up, w_down,
    ffn_norm_post, ffn1_norm_2, ffn1_w_gate_2, ffn1_w_up_2, ffn1_w_down_2, mix_norm_2,
    ffn2_norm_2, ffn2_w_gate_2, ffn2_w_up_2, ffn2_w_down_2, conv_w_pw1_2, conv_b_pw1_2,
    conv_w_dw_2, conv_b_dw_2, conv_ln_g_2, conv_ln_b_2, conv_w_pw2_2, conv_b_pw2_2, kv_norm_2,
    w_kv_2, attn_w_q_2, attn_w_o_2, final_norm_2,
):
    x = first_block(
        x, mem, rel_bias, mix_norm_pre, w_in, cmp_pos_k, cmp_pos_v, cmp_w1_k, cmp_w2_k,
        cmp_w1_v, cmp_w2_v, conv_w, conv_b, mlstm_gate_bias, mlstm_norm, w_out, mix_norm_post,
        xattn_norm_pre, mem_norm, w_xq, w_xkv, w_xo, xattn_norm_post, ffn_norm_pre, w_gate_up,
        w_down, ffn_norm_post,
    )
    return second_block(
        x, ffn1_norm_2, ffn1_w_gate_2, ffn1_w_up_2, ffn1_w_down_2, mix_norm_2, ffn2_norm_2,
        ffn2_w_gate_2, ffn2_w_up_2, ffn2_w_down_2, conv_w_pw1_2, conv_b_pw1_2, conv_w_dw_2,
        conv_b_dw_2, conv_ln_g_2, conv_ln_b_2, conv_w_pw2_2, conv_b_pw2_2, kv_norm_2, w_kv_2,
        attn_w_q_2, attn_w_o_2, final_norm_2,
    )


_drawn_inputs = setup_inputs


def setup_inputs(seed=0):
    import zlib

    import numpy as np

    out = dict(_drawn_inputs(seed))
    spreads = {}
    factors = {'cmp_pos_k': 8.0,
     'cmp_pos_v': 6.615,
     'conv_b': 5.522,
     'mlstm_norm': 3.57,
     'mix_norm_post': 3.404,
     'xattn_norm_pre': 4.263,
     'mem_norm': 2.747,
     'xattn_norm_post': 4.194,
     'ffn_norm_pre': 3.757,
     'ffn_norm_post': 5.925,
     'ffn1_norm_2': 8.0,
     'mix_norm_2': 8.0,
     'ffn2_norm_2': 8.0,
     'conv_b_pw1_2': 59.51,
     'conv_b_dw_2': 53.205,
     'conv_ln_g_2': 45.592,
     'conv_ln_b_2': 64.0,
     'conv_b_pw2_2': 61.584,
     'kv_norm_2': 26.468,
     'final_norm_2': 8.698}
    for name, (base, spread) in spreads.items():
        noise = np.random.default_rng([zlib.crc32(name.encode()), seed]).standard_normal(out[name].shape)
        drawn = base * np.exp(spread * noise) if base else spread * noise
        out[name] = __import__('jax').numpy.asarray(drawn.astype(out[name].dtype))
    for name, factor in factors.items():
        out[name] = (out[name] * factor).astype(out[name].dtype)
    return out
```

```python
import concourse.bass as bass
import numpy as np
from concourse import mybir
from contextlib import ExitStack

P = 128
D, S, MEM, DFF = 1024, 512, 256, 2816
KC = D // P
FC = DFF // P
TB = S // P
DH = 64
NCMP = S // 16 - 1
GW = 2 * NCMP + 2
TAPS = 31
PAD = TAPS - 1
NEG = -1.0e30
UNIT = KC * P
RING = 4
DN_KS = [(0, 8), (8, 8), (16, 6)]
GT, MI, MF = 0, 32, 64
HBM_BIAS = P + S

STAGES = [("in", 24, 24), ("cmp", 8, 0), ("out", 8, 8), ("xkv", 16, 16), ("xq", 8, 8), ("xo", 8, 8),
          ("gu0", 44, 44), ("dn0", 24, 8), ("gu1", 44, 44), ("dn1", 24, 8), ("pw1", 16, 16),
          ("pw2", 8, 8), ("gu2", 44, 44), ("dn2", 24, 8), ("kv", 16, 16), ("gu3", 44, 44),
          ("dn3", 24, 8), ("q", 8, 8), ("o", 8, 8), ("gu4", 44, 44), ("dn4", 24, 8)]
OPERANDS = [("mix", 8), ("cmp", 2), ("nsa", 4), ("ml", 4), ("mem", 8), ("xq", 8), ("xo", 8),
            ("gu0", 8), ("gu1", 8), ("pw1", 8), ("pw2", 8), ("gu2", 8), ("kv", 8), ("gu3", 8),
            ("q", 8), ("o", 8), ("gu4", 8)]
NORMS = [("mix", 1), ("mem", 1), ("post_mix", 1), ("xq", 1), ("post_x", 1), ("gu0", 1),
         ("post_ffn", 1), ("gu1", 1), ("pw1", 1), ("ln_mean", 0), ("ln_var", 1), ("gu2", 1),
         ("kv", 1), ("q", 1), ("gu4", 1), ("final", 1)]
VECTORS = [("mix_norm_pre", 8), ("mix_norm_post", 8), ("xattn_norm_pre", 8), ("mem_norm", 8),
           ("xattn_norm_post", 8), ("ffn_norm_pre", 8), ("ffn_norm_post", 8), ("ffn1_0", 8),
           ("ffn1_1", 8), ("mix_0", 8), ("mix_1", 8), ("ffn2_0", 8), ("ffn2_1", 8), ("kv_norm", 8),
           ("final_norm", 8), ("b_pw1", 16), ("b_dw", 8), ("ln_g", 8), ("ln_b", 8), ("b_pw2", 8),
           ("w_dw", 8 * TAPS), ("conv_w", 16), ("conv_b", 4), ("mlstm_norm", 4), ("pos_k", 16),
           ("pos_v", 16)]
CONSTS = [("ident", P), ("ones", P), ("minus_ones", P), ("mask_from_query", P), ("minus_from_here", P), ("not_after", P),
          ("pick", 4 * P), ("has_block", 1), ("one", 1), ("norm_eps", 1), ("ln_eps", 1)]


def starts(sizes):
    found, at = {}, 0
    for name, size, *_ in sizes:
        found[name], at = at, at + size
    return found, at


U0, UNITS = starts(STAGES)
B0, _ = starts([(n, b) for n, _, b in STAGES])
UEND = {n: U0[n] + k for n, k, _ in STAGES}
BEND = {n: B0[n] + b for n, _, b in STAGES}
R0, _ = starts(OPERANDS)
SQ0, _ = starts([(n, 8 * sq) for n, sq in NORMS])
ACTED0, _ = starts([("gu0", FC), ("gu1", FC), ("pw1", KC), ("gu2", FC), ("gu3", FC), ("gu4", FC)])
NORM = {n: i for i, (n, _) in enumerate(NORMS)}
VEC, NVEC = starts(VECTORS)
CST, NCST = starts(CONSTS)


def rounds(eng, n, peel=0):
    for i in range(min(peel, n)):
        yield i
    if n > peel:
        with eng.Fori(peel, n) as i:
            yield i


class Steps:

    def __init__(self, eng, sem):
        self.eng, self.sem, self.base, self.n = eng, sem, 0, 0

    def done(self, instruction):
        self.eng.wait_ge(self.sem, self.mark(instruction))

    def mark(self, instruction):
        instruction.then_inc(self.sem, 1)
        self.n += 1
        return self.base + self.n

    def loop(self, n, per, peel=0):
        first = self.base + self.n
        for i in rounds(self.eng, n, peel):
            self.base, self.n = first + i * per, 0
            yield i
            assert self.n == per, (self.n, per)
        self.base, self.n = first + n * per, 0


def block_program(nc, t, out):
    f32, f32r = mybir.dt.float32, mybir.dt.float32r
    ALU, ACT, AX = mybir.AluOpType, mybir.ActivationFunctionType, mybir.AxisListType
    mult, add, sub, amax, amin = ALU.mult, ALU.add, ALU.subtract, ALU.max, ALU.min
    ctx = ExitStack()
    with ctx:
        def held(stack):
            return lambda name, width, dt=f32: stack.enter_context(nc.sbuf_tensor(name, [P, width], dt))

        sb = held(ctx)

        def sem(name):
            return ctx.enter_context(nc.semaphore(name))

        def dram(name, shape):
            return nc.dram_tensor(name, shape, f32).ap()

        w_raw, w_hi, w_lo = sb("w_raw", RING * UNIT), sb("w_hi", RING * UNIT, f32r), sb("w_lo", RING * UNIT, f32r)
        x = sb("x", KC * S)
        vec, cst = sb("vec", NVEC), sb("cst", NCST)
        rB = sb("rB", S)
        sq, acc = sb("sq", 2 * S), sb("acc", S)
        t0, t1 = sb("t0", S), sb("t1", S)
        small = sb("small", 64)
        with ExitStack() as h:
            yb_h = held(h)("yb_h", KC * S)
        h_hi, h_lo = sb("h_hi", KC * S, f32r), sb("h_lo", KC * S, f32r)
        with ExitStack() as ph:
            a_hi, a_lo = held(ph)("a_hi", FC * S, f32r), held(ph)("a_lo", FC * S, f32r)
        with ExitStack() as ph:
            p = held(ph)
            qT, kS, kW = p("qT", 4 * S), p("kS", S), p("kW", S)
            v_nsa = p("v_nsa", TB * 2 * P)
            v_ml = p("v_ml", TB * 4 * P)
            qk, mo, gsb = p("qk", 4 * S), p("mo", 4 * S), p("gsb", S)
            gate, kc, vc = p("gate", TB * 24), p("k_cmp", NCMP + 1), p("v_cmp", P)
            cmp_h, cmp_w2, gbias = p("cmp_h", 4 * GW), p("cmp_w2", 4 * DH), p("gbias", 2)
            with ExitStack() as q:
                p2 = held(q)
                toep = p2("toep", 8 * S)
                with ExitStack() as r:
                    p3 = held(r)
                    u_pad, g_raw = p3("u_pad", 4 * (S + 3)), p3("g_raw", 16 * GW)
                    g_hi, g_lo = p3("g_hi", 2 * 16 * GW, f32r), p3("g_lo", 2 * 16 * GW, f32r)
                onehot, r_bias = qk[:, 0:S + 8], mo[:, 0:HBM_BIAS]
                with ExitStack() as r:
                    p3 = held(r)
                    q_st, s_sb, p_sb, pT = p3("q_st", S), p3("s_sb", 2 * S), p3("p_sb", 3 * S), p3("pT", 2 * S)
                    toep_st, gate_st = p3("toep_st", 2 * S), p3("gate_st", 2 * TB * 3)
            with ExitStack() as q:
                p2 = held(q)
                rows = p2("rows", 6 * S)
                a_col, decay, weight = p2("a_col", TB * 4), p2("decay", 2 * S), p2("weight", 2 * S)
                diag, floor, h_ml = p2("diag", 2 * P), p2("floor", S), p2("h_ml", 4 * S)
        with ExitStack() as ph:
            p = held(ph)
            yb_x, mem, rM = p("yb_x", KC * S), p("mem", KC * MEM), p("rM", MEM)
            m_hi, m_lo = p("m_hi", KC * MEM, f32r), p("m_lo", KC * MEM, f32r)
            kx, vx, qx = p("kx", KC * MEM), p("vx", 2 * D), p("qx", KC * S)
            px, pxT = p("px", 3 * MEM), p("pxT", 2 * 2 * S)
        with ExitStack() as ph:
            p = held(ph)
            o_hi, o_lo = p("o_hi", KC * S, f32r), p("o_lo", KC * S, f32r)
            with ExitStack() as q:
                u_conv, cv = held(q)("u_conv", KC * (S + PAD)), held(q)("cv", KC * S)
            with ExitStack() as q:
                p2 = held(q)
                qkv, v_st = p2("qkv", 2 * 3 * S), p2("v_st", 2 * S)
                s_e, s_l, s_w = p2("s_e", 2 * S), p2("s_l", 2 * TB * S), p2("s_w", 2 * S)
        bank = [ctx.enter_context(nc.psum_tensor(f"bank{i}", [P, 4 * S], f32)) for i in range(2)]
        bank = [bank[i // 4][:, (i % 4) * S:(i % 4 + 1) * S] for i in range(8)]
        bias_dram, qkv_dram = dram("bias_by_distance", (8, HBM_BIAS)), dram("stick_qkv", (KC, P, 3, S))

        raw_in = [sem(f"raw_in{i}") for i in range(RING)]
        w_hi_made, w_lo_made = sem("w_hi_made"), sem("w_lo_made")
        w_used = sem("w_used")
        evacuated = sem("evacuated")
        op_hi, op_lo = sem("op_hi"), sem("op_lo")
        f_hi, f_lo = sem("f_hi"), sem("f_lo")
        squared, summed = sem("squared"), sem("summed")
        stat_done, root_done, r_done = sem("stat_done"), sem("root_done"), sem("r_done")
        loaded, x_in, mem_in = sem("loaded"), sem("x_in"), sem("mem_in")
        posted = sem("posted")
        acted, inner_made, acted_mix, m_out = (sem(n) for n in ("acted", "inner_made", "acted_mix", "ml_out"))
        dve_step, act_step, pe_step = sem("dve_step"), sem("act_step"), sem("pe_step")
        spilled, fetched = ([sem(f"{n}{i}") for i in range(2)] for n in ("spilled", "fetched"))
        rel_in, bias_psum, bias_sb, bias_out, toep_in = (sem(n) for n in ("rel_in", "bias_psum", "bias_sb", "bias_out", "toep_in"))
        v_ready, v_turned, v_stored = sem("v_ready"), sem("v_turned"), sem("v_stored")
        conv_in, gates_in, gates_turned, gates_out = (sem(n) for n in ("conv_in", "gates_in", "gates_turned", "gates_out"))
        gathered, hid_done, hid_bias, hid_act, cmp_proj, cmp_out = (sem(n) for n in ("gathered", "hid_done", "hid_bias", "hid_act", "cmp_proj", "cmp_out"))
        n_q, n_qk, n_add, n_exp, n_scaled, n_turned, n_pT, n_pv = (sem("nsa_" + n) for n in ("q", "qk", "add", "exp", "scaled", "turned", "pT", "pv"))
        m_row, m_col, m_colout, m_bc, m_floor, m_qk, m_diag, m_decay, m_weight, m_pv, m_h, m_sq, m_sum, m_root = (
            sem("ml_" + n) for n in ("row", "col", "colout", "bc", "floor", "qk", "diag", "decay", "weight", "pv", "h", "sq", "sum", "root"))
        m_soft, n_seen = sem("ml_soft"), sem("nsa_seen")
        x_qk, x_max, x_exp, x_scaled, x_turned, x_pT, x_pv = (sem("x_" + n) for n in ("qk", "max", "exp", "scaled", "turned", "pT", "pv"))
        c_conv, c_cent, c_norm = (sem("c_" + n) for n in ("conv", "cent", "norm"))
        s_v, s_vout, s_qk, s_clip, s_soft, s_log, s_sum, s_wt, s_pv = (
            sem("st_" + n) for n in ("v", "vout", "qk", "clip", "soft", "log", "sum", "wt", "pv"))
        last_out, out_done, w2_in = sem("last_out"), sem("out_done"), sem("w2_in")
        gb_in, bias_fill, pad_done, gather_part, gates_part, m_abs = (sem(n) for n in ("gb_in", "bias_fill", "pad_done", "gather_part", "gates_part", "ml_abs"))

        def cut(tile, k, w=S):
            return tile[:, bass.ds(k * w, w)]

        def col(name, c=0):
            return vec[:, bass.ds(c + VEC[name], 1)]

        def const(name, rows=P, lo=0, hi=None):
            size = dict(CONSTS)[name]
            return cst[0:rows, CST[name] + lo:CST[name] + (size if hi is None else hi)]

        ident = const("ident")
        stage_blocks = {n: b for n, _, b in STAGES}
        V_IN = [8, 9, 10, 11, 12, 13]

        block = ctx.enter_context(nc.Block())

        @block.sync
        def _(sp):
            sp.dma_start(vec[:], t["vectors"]).then_inc(loaded, 16)
            sp.dma_start(cst[:], t["consts"]).then_inc(loaded, 16)
            sp.dma_start(x[:], t["x"].rearrange("p c n -> p (c n)")).then_inc(x_in, 16)

            def load(slot, src, q):
                u = 4 * q + slot
                if not (isinstance(q, int) and u < RING):
                    sp.wait_ge(w_lo_made, u - 3)
                width = src.shape[-1]
                sp.dma_start(w_raw[:, slot * UNIT:slot * UNIT + width], src).then_inc(raw_in[slot], 16)

            def flat(w):
                return w.rearrange("u p k n -> u p (k n)")

            def stage(name, w):
                w = flat(w)
                q0 = U0[name] // RING
                for it in rounds(sp, w.shape[0] // RING):
                    for j in range(RING):
                        load(j, w[bass.ds(RING * it + j, 1)].rearrange("u p n -> (u p) n"), q0 + it)

            def stage_down(name, w):
                w = flat(w)
                q0 = U0[name] // RING
                for it in rounds(sp, KC // 4):
                    for j in range(12):
                        k0, kn = DN_KS[j % 3]
                        src = w[bass.ds(4 * it + j // 3, 1), :, k0 * P:(k0 + kn) * P].rearrange("u p n -> (u p) n")
                        load(j % RING, src, q0 + 3 * it + j // RING)

            w_in = flat(t["w_in"])
            for u in range(22):
                load(u % RING, w_in[u], u // RING)
            for j in range(2):
                load(2 + j, t["w_gates"].rearrange("p k n -> p (k n)")[:, j * 4 * P:(j + 1) * 4 * P], 5)
            stage("cmp", t["cmp_w1"])
            stage("out", t["w_out"])
            stage("xkv", t["w_xkv"])
            stage("xq", t["w_xq"])
            stage("xo", t["w_xo"])
            stage("gu0", t["w_gu0"])
            stage_down("dn0", t["w_dn0"])
            stage("gu1", t["w_gu1"])
            stage_down("dn1", t["w_dn1"])
            stage("pw1", t["w_pw1"])
            stage("pw2", t["w_pw2"])
            stage("gu2", t["w_gu2"])
            stage_down("dn2", t["w_dn2"])
            stage("kv", t["w_kv"])
            stage("gu3", t["w_gu3"])
            stage_down("dn3", t["w_dn3"])
            stage("q", t["w_q"])
            w_o = flat(t["w_o"])
            for u in range(RING):
                load(u, w_o[u], U0["o"] // RING)
            for par in range(2):
                sp.wait_ge(spilled[par], 16 * 12)
            for it in rounds(sp, KC // 2):
                for j in range(2):
                    sp.wait_ge(op_lo, R0["o"] + 2 * it + j - 1)
                    sp.dma_start(qkv[:, j * 3 * S:(j + 1) * 3 * S],
                                 qkv_dram[bass.ds(2 * it + j, 1)].rearrange("c p a n -> (c p) (a n)")).then_inc(fetched[j], 16)
            for u in range(RING, KC):
                load(u - RING, w_o[u], U0["o"] // RING + 1)
            stage("gu4", t["w_gu4"])
            stage_down("dn4", t["w_dn4"])

        @block.tensor
        def _(pe):
            def unit(q, j, dst, ks, hi, lo, start, stop, n=S, made=None, wait=op_lo):
                slot, q = j % RING, q + j // RING
                pe.wait_ge(w_lo_made, 4 * q + slot + 1)
                for i, k in enumerate(ks):
                    if made is not None:
                        pe.wait_ge(wait, made + k + 1)
                    at = slot * UNIT + i * P
                    parts = ((w_hi, hi), (w_lo, hi), (w_hi, lo))
                    for m, (w, o) in enumerate(parts):
                        last = nc.tensor.matmul(dst[:, 0:n], w[:, at:at + P], o[:, k * n:(k + 1) * n],
                                                start=start and i == 0 and m == 0,
                                                stop=stop and i == len(ks) - 1 and m == 2)
                last.then_inc(w_used, 1)

            def bank_free(b):
                if not (isinstance(b, int) and b < 4):
                    pe.wait_ge(evacuated, b - 3)

            def feature_sum(name, n=S):
                pe.wait_ge(summed, 9 * NORM[name] + 9)
                nc.tensor.matmul(bank[7][:, 0:n], const("ones"), acc[:, 0:n], start=True, stop=True).then_inc(stat_done, 1)

            def dense(name, hi, lo, operand, norm=None, n=S):
                for it in rounds(pe, stage_blocks[name] // 4, peel=1):
                    for j in range(4):
                        bank_free(B0[name] + 4 * it + j)
                        first = isinstance(it, int) and it == 0 and j == 0
                        unit(U0[name] // 4 + it, j, bank[j], range(KC), hi, lo, True, True, n,
                             made=R0[operand] if first else None)
                        if first and norm:
                            feature_sum(norm, n)

            def down(name, f):
                for it in rounds(pe, KC // 4, peel=1):
                    for j in range(12):
                        b, r = divmod(j, 3)
                        k0, kn = DN_KS[r]
                        if r == 0:
                            bank_free(B0[name] + 4 * it + b)
                        first = isinstance(it, int) and it == 0 and b == 0
                        unit(U0[name] // 4 + 3 * it, j, bank[b], range(k0, k0 + kn), a_hi, a_lo, r == 0, r == 2,
                             made=FC * f if first else None, wait=f_lo)

            pe.wait_ge(rel_in, 16)
            pe.wait_ge(loaded, 32)
            nc.tensor.matmul(bank[6][0:8, 0:S], onehot[0:32, S:S + 8], onehot[0:32, 0:S], start=True,
                             stop=True).then_inc(bias_psum, 1)

            idx = 0
            for b in range(22):
                bank_free(b)
                unit(b // 4, b % 4, bank[b % 4], range(KC), h_hi, h_lo, True, True, made=R0["mix"] if b == 0 else None)
                if b == 0:
                    feature_sum("mix")
                if b - 1 in V_IN:
                    pe.wait_ge(v_ready, idx + 1)
                    if idx >= 2:
                        pe.wait_ge(v_stored, idx - 1)
                    if idx == 1:
                        pe.wait_ge(bias_sb, 1)
                    src = (t0, t1)[idx % 2]
                    for k in range(TB):
                        last = nc.tensor.transpose(bank[5 + idx % 2][:, k * P:(k + 1) * P], src[:, k * P:(k + 1) * P], ident)
                    last.then_inc(v_turned, 1)
                    idx += 1
            bank_free(22)
            for j in range(2):
                slot = 2 + j
                pe.wait_ge(w_lo_made, 22 + j + 1)
                for i in range(4):
                    k = 4 * j + i
                    at = slot * UNIT + i * P
                    for m, (w, o) in enumerate(((w_hi, h_hi), (w_lo, h_hi), (w_hi, h_lo))):
                        last = nc.tensor.matmul(bank[2][:], w[:, at:at + P], cut(o, k), start=k == 0 and m == 0,
                                                stop=k == 7 and m == 2)
                last.then_inc(w_used, 1)
            pe.wait_ge(gates_in, 1)
            for k in range(TB):
                last = nc.tensor.transpose(bank[5][:, k * 24:(k + 1) * 24], gsb[0:24, k * P:(k + 1) * P], ident[0:24, 0:24])
            last.then_inc(gates_turned, 1)

            pe.wait_ge(evacuated, BEND["in"])
            for w in range(2):
                pe.wait_ge(op_lo, R0["cmp"] + w + 1)
                for uu in range(4):
                    pe.wait_ge(w_lo_made, U0["cmp"] + 4 * w + uu + 1)
                    for i in range(4):
                        g = (w * 16 + 4 * uu + i) * GW
                        for f in range(2):
                            at = uu * UNIT + (2 * i + f) * P
                            for m, (ww, o) in enumerate(((w_hi, g_hi), (w_lo, g_hi), (w_hi, g_lo))):
                                last = nc.tensor.matmul(bank[2 * w + f][:, 0:GW], ww[:, at:at + P], o[:, g:g + GW],
                                                        start=uu == 0 and i == 0 and m == 0,
                                                        stop=uu == 3 and i == 3 and m == 2)
                    last.then_inc(w_used, 1)
            w2 = lambda w, f: cmp_w2[:, (2 * w + f) * DH:(2 * w + f + 1) * DH]
            hid = lambda w, f, h: cmp_h[:, (2 * w + f) * GW + h * NCMP:(2 * w + f) * GW + (h + 1) * NCMP]
            pe.wait_ge(hid_act, 2)
            pe.wait_ge(w2_in, 16)
            for h in range(2):
                for f in range(2):
                    nc.tensor.matmul(bank[4][h * DH:(h + 1) * DH, 0:NCMP], w2(0, f), hid(0, f, h), start=f == 0, stop=f == 1)
            pe.wait_ge(hid_act, 4)
            pe.wait_ge(gates_out, 1)
            for h in range(2):
                for f in range(2):
                    last = nc.tensor.matmul(bank[5][0:NCMP, h * DH:(h + 1) * DH], hid(1, f, h), w2(1, f), start=f == 0, stop=f == 1)
            last.then_inc(cmp_proj, 1)

            pe.wait_ge(cmp_out, 2)
            items = [(half, qb, br) for half in range(2) for qb in range(TB) for br in range(3)]
            NI = len(items)
            for c in rounds(pe, 4):
                pe.wait_ge(n_q, c + 1)
                for s in range(NI + 3):
                    if s < NI:
                        half, qb, br = items[s]
                        rs = slice(half * DH, (half + 1) * DH)
                        n = (8 * qb + 7) if br == 0 else P * (qb + 1)
                        if s >= 2:
                            pe.wait_ge(n_add, NI * c + s - 1)
                        nc.tensor.matmul(bank[s % 2][:, 0:n], q_st[rs, qb * P:(qb + 1) * P],
                                         (kc, kS, kW)[br][rs, 0:n], start=True, stop=True).then_inc(n_qk, 1)
                    r = s - 2
                    if 0 <= r < NI:
                        half, qb, br = items[r]
                        pe.wait_ge(n_scaled, NI * c + r + 1)
                        if r >= 2:
                            pe.wait_ge(n_pT, NI * c + r - 1)
                        src, dst = p_sb[:, (r % 3) * S:(r % 3 + 1) * S], bank[2 + r % 2]
                        if br == 0:
                            n = 8 * qb + 7
                            last = nc.tensor.transpose(dst[0:n, 0:P], src[:, 0:n], ident)
                        else:
                            for k in range(qb + 1):
                                last = nc.tensor.transpose(dst[:, k * P:(k + 1) * P], src[:, k * P:(k + 1) * P], ident)
                        last.then_inc(n_turned, 1)
                    r = s - 3
                    if 0 <= r < NI:
                        half, qb, br = items[r]
                        pe.wait_ge(n_pT, NI * c + r + 1)
                        if r == 0:
                            pe.wait_ge(op_lo, R0["nsa"] + c)
                        dst = bank[4][half * DH:(half + 1) * DH, qb * P:(qb + 1) * P]
                        src = pT[:, (r % 2) * S:(r % 2 + 1) * S]
                        if br == 0:
                            n = 8 * qb + 7
                            last = nc.tensor.matmul(dst, vc[0:n, half * DH:(half + 1) * DH], src[0:n, 0:P], start=True, stop=False)
                        else:
                            for k in range(qb + 1):
                                at = k * 2 * P + (br - 1) * P + half * DH
                                last = nc.tensor.matmul(dst, v_nsa[:, at:at + DH], src[:, k * P:(k + 1) * P], start=False,
                                                        stop=br == 2 and k == qb)
                        last.then_inc(n_pv, 1)

            pe.wait_ge(m_row, 1)
            pe.wait_ge(acted_mix, 8)
            pe.wait_ge(op_lo, R0["nsa"] + 4)
            for k in range(TB):
                last = nc.tensor.transpose(bank[2][:, 4 * k:4 * k + 4], rows[0:4, k * P:(k + 1) * P], ident[0:4, 0:4])
            last.then_inc(m_col, 1)
            pe.wait_ge(m_colout, 1)

            def ml_values(i):
                hd, kb = divmod(i, TB)
                pe.wait_ge(m_weight, i + 1)
                if kb == 0 and hd >= 2:
                    pe.wait_ge(m_h, hd - 1)
                n = S - kb * P
                src = weight[:, (i % 2) * S:(i % 2) * S + n]
                at = kb * 4 * P + hd * P
                nc.tensor.matmul(bank[4 + hd % 2][:, kb * P:S], v_ml[:, at:at + P], src, start=kb == 0, stop=kb == 3)
                nc.tensor.matmul(bank[6 + hd % 2][:, kb * P:S], const("ones"), src, start=kb == 0,
                                 stop=kb == 3).then_inc(m_pv, 1)

            for i in range(16):
                hd, kb = divmod(i, TB)
                if kb == 0:
                    if hd:
                        pe.wait_ge(m_decay, 4 * hd)
                        pe.wait_ge(m_floor, hd)
                    pick = const("pick", 4, hd * P, (hd + 1) * P)
                    nc.tensor.matmul(bank[0][:], pick, rows[0:4, 2 * S:3 * S], start=True, stop=True)
                    nc.tensor.matmul(bank[1][:], pick, rows[0:4, 3 * S:4 * S], start=True, stop=True).then_inc(m_bc, 1)
                if i >= 2:
                    pe.wait_ge(m_weight, i - 1)
                rs = slice((hd % 2) * DH, (hd % 2 + 1) * DH)
                k_at, q_at = (2 + hd // 2) * S + kb * P, (hd // 2) * S
                nc.tensor.matmul(bank[2 + i % 2][:, 0:S - kb * P], qk[rs, k_at:k_at + P], qk[rs, q_at + kb * P:q_at + S],
                                 start=True, stop=True).then_inc(m_qk, 1)
                if i >= 1:
                    ml_values(i - 1)
            ml_values(15)
            pe.wait_ge(m_h, 4)
            for hd in range(4):
                pe.wait_ge(m_sq, hd + 1)
                nc.tensor.matmul(bank[hd][:], const("ones"), cut(rows, hd), start=True, stop=True).then_inc(m_sum, 1)
            for it in rounds(pe, 2, peel=1):
                for j in range(4):
                    bank_free(B0["out"] + 4 * it + j)
                    first = isinstance(it, int) and it == 0 and j == 0
                    if first:
                        pe.wait_ge(op_lo, R0["ml"] + 4)
                    unit(U0["out"] // 4 + it, j, bank[j], range(KC), h_hi, h_lo, True, True)
                    if first:
                        feature_sum("mem", MEM)
            for it in range(2):
                for j in range(4):
                    bank_free(B0["xkv"] + 4 * it + j)
                    unit(U0["xkv"] // 4 + it, j, bank[j], range(KC), m_hi, m_lo, True, True, MEM,
                         made=R0["mem"] if it == 0 and j == 0 else None)
                    if it == 0 and j == 0:
                        feature_sum("post_mix")
            for it in rounds(pe, 2):
                for j in range(5):
                    if j < 4:
                        bank_free(B0["xkv"] + 8 + 4 * it + j)
                        unit(U0["xkv"] // 4 + 2 + it, j, bank[j], range(KC), m_hi, m_lo, True, True, MEM)
                    if j:
                        i = 6 + 4 * it + j - 1
                        pe.wait_ge(v_ready, i + 1)
                        pe.wait_ge(v_stored, i - 1)
                        for k in range(2):
                            last = nc.tensor.transpose(bank[5 + (j - 1) % 2][:, k * P:(k + 1) * P],
                                                       (t0, t1)[(j - 1) % 2][:, k * P:(k + 1) * P], ident)
                        last.then_inc(v_turned, 1)
            dense("xq", h_hi, h_lo, "xq", "xq")
            pe.wait_ge(evacuated, BEND["xq"])
            pe.wait_ge(v_stored, 14)
            for s in range(16 + 2):
                if s < 16:
                    hd, qb = divmod(s, TB)
                    if s >= 2:
                        pe.wait_ge(x_exp, s - 1)
                    for k in range(2):
                        last = nc.tensor.matmul(bank[s % 2][:, 0:MEM], qx[:, (2 * hd + k) * S + qb * P:(2 * hd + k) * S + (qb + 1) * P],
                                                cut(kx, 2 * hd + k, MEM), start=k == 0, stop=k == 1)
                    last.then_inc(x_qk, 1)
                r = s - 2
                if r >= 0:
                    hd, qb = divmod(r, TB)
                    pe.wait_ge(x_scaled, r + 1)
                    if r >= 2:
                        pe.wait_ge(x_pT, r - 1)
                    for k in range(2):
                        last = nc.tensor.transpose(bank[2 + r % 2][:, k * P:(k + 1) * P],
                                                   px[:, (r % 3) * MEM + k * P:(r % 3) * MEM + (k + 1) * P], ident)
                    last.then_inc(x_turned, 1)
                    if qb == 3:
                        pe.wait_ge(x_pT, r + 1)
                        for dv in range(2):
                            c = 2 * hd + dv
                            if c >= 2:
                                pe.wait_ge(op_lo, R0["xo"] + c - 1)
                            for k in range(2):
                                last = nc.tensor.matmul(bank[4 + dv][:], vx[:, k * D + c * P:k * D + (c + 1) * P],
                                                        pxT[:, ((hd % 2) * 2 + k) * S:((hd % 2) * 2 + k + 1) * S],
                                                        start=k == 0, stop=k == 1)
                            last.then_inc(x_pv, 1)
            dense("xo", h_hi, h_lo, "xo")
            feature_sum("post_x")
            dense("gu0", h_hi, h_lo, "gu0", "gu0")
            down("dn0", 0)
            feature_sum("post_ffn")
            dense("gu1", h_hi, h_lo, "gu1", "gu1")
            down("dn1", 1)
            dense("pw1", h_hi, h_lo, "pw1", "pw1")
            feature_sum("ln_mean")
            feature_sum("ln_var")
            dense("pw2", o_hi, o_lo, "pw2")
            dense("gu2", h_hi, h_lo, "gu2", "gu2")
            down("dn2", 2)
            dense("kv", h_hi, h_lo, "kv", "kv")
            dense("gu3", h_hi, h_lo, "gu3")
            down("dn3", 3)
            dense("q", h_hi, h_lo, "q", "q")

            pe.wait_ge(evacuated, BEND["q"])
            sticks = [(half, kb) for half in range(2) for kb in reversed(range(TB))]
            for it in rounds(pe, KC // 2):
                for j in range(2):
                    pe.wait_ge(fetched[j], 16 * (it + 1))
                    kT, qT_, vT = (qkv[:, (3 * j + m) * S:(3 * j + m + 1) * S] for m in (1, 0, 2))
                    for k in range(TB):
                        last = nc.tensor.transpose(bank[5][:, k * P:(k + 1) * P], vT[:, k * P:(k + 1) * P], ident)
                    last.then_inc(s_v, 1)
                    for s in range(8 + 4):
                        base = 16 * it + 8 * j
                        if s < 8:
                            half, kb = sticks[s]
                            rs = slice(half * DH, (half + 1) * DH)
                            if s >= 4:
                                pe.wait_ge(s_wt, base + s - 3)
                            nc.tensor.matmul(bank[s % 4][:, 0:S - kb * P], kT[rs, kb * P:(kb + 1) * P], qT_[rs, kb * P:S],
                                             start=True, stop=False, skip_group_check=True)
                            nc.tensor.matmul(bank[s % 4][:, 0:P], const("mask_from_query"), ident, start=False, stop=False,
                                             skip_group_check=True).then_inc(s_qk, 1)
                        r = s - 2
                        if 0 <= r < 8:
                            half, kb = sticks[r]
                            n = S - kb * P
                            pe.wait_ge(s_soft, base + r + 1)
                            l_at = lambda k: (half * TB + k) * S
                            dst = bank[r % 4]
                            last = nc.tensor.matmul(dst[:, 0:n], const("minus_from_here"), s_l[:, l_at(kb):l_at(kb) + n],
                                                    start=False, stop=kb == 3, skip_group_check=True)
                            for k in range(kb + 1, TB):
                                last = nc.tensor.matmul(dst[:, (k - kb) * P:n], const("minus_ones"), s_l[:, l_at(k):l_at(k) + S - k * P],
                                                        start=False, stop=k == 3, skip_group_check=True)
                            last.then_inc(s_sum, 1)
                        r = s - 4
                        if r >= 0:
                            half, kb = sticks[r]
                            n = S - kb * P
                            pe.wait_ge(s_wt, base + r + 1)
                            if r == 0:
                                pe.wait_ge(s_vout, 2 * it + j + 1)
                                pe.wait_ge(op_lo, R0["o"] + 2 * it + j)
                            lhs = v_st[:, j * S + kb * P + half * DH:j * S + kb * P + half * DH + DH]
                            src = s_w[:, (r % 2) * S:(r % 2) * S + n]
                            dst = bank[4][half * DH:(half + 1) * DH, :]
                            last = nc.tensor.matmul(dst[:, kb * P:(kb + 1) * P], lhs, src[:, 0:P], start=kb == 3, stop=kb == 0,
                                                    skip_group_check=True)
                            if kb < 3:
                                last = nc.tensor.matmul(dst[:, (kb + 1) * P:S], lhs, src[:, P:n], start=False, stop=kb == 0,
                                                        skip_group_check=True)
                            last.then_inc(s_pv, 1)
            dense("o", o_hi, o_lo, "o")
            dense("gu4", h_hi, h_lo, "gu4", "gu4")
            down("dn4", 4)
            feature_sum("final")

        @block.scalar
        def _(act):
            steps = Steps(act, act_step)

            def split(name, it, per, j):
                q, slot = U0[name] // RING + it * (per // RING) + j // RING, j % RING
                if isinstance(q, int) and 4 * q + slot >= UNITS:
                    return
                act.wait_ge(raw_in[slot], 16 * (q + 1))
                if not (isinstance(q, int) and q == 0):
                    act.wait_ge(w_used, 4 * q + slot - 3)
                nc.scalar.activation(cut(w_hi, slot, UNIT), cut(w_raw, slot, UNIT), ACT.Copy).then_inc(w_hi_made, 1)

            def chunk(norm, c, k, gain, src=x, hi=h_hi, n=S):
                if not (isinstance(c, int) and c == 0 and NORM[norm] == 0):
                    act.wait_ge(summed, 9 * NORM[norm] + c)
                nc.scalar.activation(sq[:, (k % 2) * S:(k % 2) * S + n], cut(src, c, n), ACT.Square).then_inc(squared, 1)
                if gain is not None:
                    nc.scalar.activation(cut(hi, c, n), cut(src, c, n), ACT.Copy, scale=col(gain, c)).then_inc(op_hi, 1)

            def root(name, dst=rB, n=S, eps="norm_eps"):
                act.wait_ge(stat_done, NORM[name] + 1)
                nc.scalar.activation(dst[:, 0:n], bank[7][:, 0:n], ACT.Sqrt, scale=1.0 / D, bias=const(eps)).then_inc(root_done, 1)

            def stage(name, norm=None, after=None, per=4, peel=0):
                n_it = (UEND[name] - U0[name]) // per
                for it in rounds(act, n_it, peel=max(peel, 1 if norm else 0)):
                    for j in range(per):
                        split(name, it, per, j + 2)
                        if isinstance(it, int) and it == 0 and j == 0 and norm:
                            root(norm)
                        if after:
                            after(it, j)

            def gate_up(name, f, norm):
                def inner(it, j):
                    if j % 2:
                        c = 2 * it + j // 2
                        act.wait_ge(evacuated, B0[name] + 4 * it + j)
                        nc.scalar.activation(t0[:], t0[:], ACT.Silu).then_inc(acted, 1)
                        act.wait_ge(inner_made, FC * f + c + 1)
                        nc.scalar.activation(cut(a_hi, c), t1[:], ACT.Copy).then_inc(f_hi, 1)
                stage(name, norm, inner)

            def down(name, norm, gain, src=x):
                def result(it, j):
                    if j % 3 == 2:
                        c = 4 * it + j // 3
                        act.wait_ge(evacuated, B0[name] + c + 1)
                        chunk(norm, c, j // 3, gain, src)
                stage(name, None, result, per=12, peel=2 if name == "dn4" else 0)

            def post(norm, base, gain):
                for c in range(KC):
                    act.wait_ge(posted, base + c + 1)
                    chunk(norm, c, c, gain)

            for j in range(2):
                split("in", 0, 4, j)
            act.wait_ge(loaded, 32)
            act.wait_ge(x_in, 16)
            for c in range(KC):
                chunk("mix", c, c, "mix_norm_pre")

            for u in range(24):
                split("in", 0, 4, u + 2)
                if u == 0:
                    root("mix")
                b = u - 1
                if b in (4, 5):
                    w = b - 4
                    act.wait_ge(gathered, w + 1)
                    nc.scalar.activation(g_hi[:, w * 16 * GW:(w + 1) * 16 * GW], g_raw[:], ACT.Copy).then_inc(op_hi, 1)
                if 14 <= b < 18:
                    act.wait_ge(conv_in, b - 13)
                    nc.scalar.activation(cut(qk, b - 14), cut(qk, b - 14), ACT.Silu, bias=col("conv_b", b - 14)).then_inc(acted_mix, 1)
                if 18 <= b < 22:
                    act.wait_ge(evacuated, b + 1)
                    nc.scalar.activation(cut(mo, b - 18), cut(mo, b - 18), ACT.Sigmoid).then_inc(acted_mix, 1)
            act.wait_ge(evacuated, BEND["in"])
            nc.scalar.activation(gsb[0:24, :], gsb[0:24, :], ACT.Sigmoid).then_inc(gates_in, 1)

            def hidden(w):
                for f in range(2):
                    act.wait_ge(hid_bias, 2 * w + f + 1)
                    at = (2 * w + f) * GW
                    nc.scalar.activation(cmp_h[:, at:at + 2 * NCMP], bank[2 * w + f][:, 0:2 * NCMP], ACT.Silu,
                                         bias=small[:, 2 * w + f:2 * w + f + 1]).then_inc(hid_act, 1)

            for u in range(8):
                split("cmp", 0, 4, u + 2)
                if u == 5:
                    hidden(0)
            hidden(1)

            items = [(half, qb, br) for half in range(2) for qb in range(TB) for br in range(3)]
            NI = len(items)
            for c in rounds(act, 4):
                for s in range(NI + 2):
                    if s < NI:
                        half, qb, br = items[s]
                        n = (8 * qb + 7) if br == 0 else P * (qb + 1)
                        act.wait_ge(n_add, NI * c + s + 1)
                        if s >= 3:
                            act.wait_ge(n_turned, NI * c + s - 2)
                        nc.scalar.activation(p_sb[:, (s % 3) * S:(s % 3) * S + n], s_sb[:, (s % 2) * S:(s % 2) * S + n], ACT.Exp,
                                             scale=-1.0, bias=small[:, 8 + s % 2:9 + s % 2],
                                             accum_out=small[:, 12 + s % 2:13 + s % 2]).then_inc(n_exp, 1)
                    r = s - 2
                    if r >= 0:
                        half, qb, br = items[r]
                        act.wait_ge(n_turned, NI * c + r + 1)
                        if r >= 2:
                            act.wait_ge(n_pv, NI * c + r - 1)
                        rows_n, n = (8 * qb + 7, P) if br == 0 else (P, P * (qb + 1))
                        nc.scalar.activation(pT[0:rows_n, (r % 2) * S:(r % 2) * S + n], bank[2 + r % 2][0:rows_n, 0:n],
                                             ACT.Copy).then_inc(n_pT, 1)
                act.wait_ge(n_pv, NI * c + NI)
                nc.scalar.activation(cut(h_hi, c), bank[4][:], ACT.Copy).then_inc(op_hi, 1)

            act.wait_ge(m_abs, 2)
            steps.done(nc.scalar.activation(rows[0:4, 4 * S:5 * S], rows[0:4, 4 * S:5 * S], ACT.Exp, scale=-1.0))
            nc.scalar.activation(rows[0:4, 4 * S:5 * S], rows[0:4, 4 * S:5 * S], ACT.Ln, bias=const("one", 4)).then_inc(m_soft, 1)
            for i in range(16):
                hd, kb = divmod(i, TB)
                dst = decay[:, (i % 2) * S:(i % 2 + 1) * S]
                if i >= 2:
                    act.wait_ge(m_weight, i - 1)
                act.wait_ge(m_diag, i + 1)
                last = nc.scalar.activation(dst[:, 0:P], diag[:, (i % 2) * P:(i % 2 + 1) * P], ACT.Exp)
                if kb < 3:
                    last = nc.scalar.activation(dst[:, P:S - kb * P], bank[0][:, (kb + 1) * P:S], ACT.Exp,
                                                bias=a_col[:, 4 * kb + hd:4 * kb + hd + 1])
                last.then_inc(m_decay, 1)
                if kb == 3:
                    if hd:
                        act.wait_ge(m_h, hd)
                    nc.scalar.activation(floor[:], bank[1][:], ACT.Exp).then_inc(m_floor, 1)
            act.wait_ge(m_h, 4)
            for hd in range(4):
                nc.scalar.activation(cut(rows, hd), cut(h_ml, hd), ACT.Square).then_inc(m_sq, 1)
            act.wait_ge(m_sum, 4)
            for hd in range(4):
                nc.scalar.activation(cut(rows, hd), bank[hd][:], ACT.Sqrt, scale=1.0 / P, bias=const("norm_eps")).then_inc(m_root, 1)
            for hd in range(4):
                act.wait_ge(m_out, hd + 1)
                nc.scalar.activation(cut(h_hi, 4 + hd), cut(h_ml, hd), ACT.Copy).then_inc(op_hi, 1)
            act.wait_ge(mem_in, 16)
            for c in range(KC):
                chunk("mem", c, c, "mem_norm", mem, m_hi, MEM)

            for u in range(8):
                split("out", 0, 4, u + 2)
                if u == 0:
                    root("mem", rM, MEM)
                act.wait_ge(evacuated, B0["out"] + u + 1)
                chunk("post_mix", u, u, None, yb_x)

            for u in range(8):
                split("xkv", 0, 4, u + 2)
                if u == 0:
                    root("post_mix")
                act.wait_ge(posted, u + 1)
                chunk("xq", u, u, "xattn_norm_pre")
            for it in rounds(act, 2):
                for j in range(4):
                    split("xkv", it + 2, 4, j + 2)
            stage("xq", "xq")
            for s in range(16 + 2):
                if s < 16:
                    if s >= 3:
                        act.wait_ge(x_turned, s - 2)
                    act.wait_ge(x_max, s + 1)
                    nc.scalar.activation(cut(px, s % 3, MEM), bank[s % 2][:, 0:MEM], ACT.Exp, bias=small[:, 8 + s % 2:9 + s % 2],
                                         accum_out=small[:, 12 + s % 2:13 + s % 2]).then_inc(x_exp, 1)
                r = s - 2
                if r >= 0:
                    hd, qb = divmod(r, TB)
                    act.wait_ge(x_turned, r + 1)
                    if qb == 0 and hd >= 2:
                        act.wait_ge(x_pv, 2 * hd - 2)
                    for k in range(2):
                        at = ((hd % 2) * 2 + k) * S + qb * P
                        last = nc.scalar.activation(pxT[:, at:at + P], bank[2 + r % 2][:, k * P:(k + 1) * P], ACT.Copy)
                    last.then_inc(x_pT, 1)
                    if qb == 3:
                        for dv in range(2):
                            act.wait_ge(x_pv, 2 * hd + dv + 1)
                            nc.scalar.activation(cut(h_hi, 2 * hd + dv), bank[4 + dv][:], ACT.Copy).then_inc(op_hi, 1)

            def result_yb(it, j):
                act.wait_ge(evacuated, B0["xo"] + 4 * it + j + 1)
                chunk("post_x", 4 * it + j, j, None, yb_x)
            stage("xo", None, result_yb)
            root("post_x")
            post("gu0", 8, "ffn_norm_pre")
            gate_up("gu0", 0, "gu0")
            down("dn0", "post_ffn", None, yb_h)
            root("post_ffn")
            post("gu1", 16, "ffn1_0")
            gate_up("gu1", 1, "gu1")
            down("dn1", "pw1", "mix_0")

            def glu(it, j):
                if j % 2:
                    act.wait_ge(evacuated, B0["pw1"] + 4 * it + j + 1)
                    nc.scalar.activation(t0[:], t0[:], ACT.Sigmoid, bias=col("b_pw1", 8 + 2 * it + j // 2)).then_inc(acted, 1)
            stage("pw1", "pw1", glu)
            act.wait_ge(stat_done, NORM["ln_mean"] + 1)
            nc.scalar.activation(rB[:], bank[7][:], ACT.Copy, scale=1.0 / D).then_inc(root_done, 1)
            for c in range(KC):
                act.wait_ge(c_cent, c + 1)
                chunk("ln_var", c, c, None, cv)
            root("ln_var", eps="ln_eps")
            for c in range(KC):
                act.wait_ge(c_norm, c + 1)
                steps.done(nc.scalar.activation(cut(cv, c), cut(cv, c), ACT.Silu, scale=col("ln_g", c), bias=col("ln_b", c)))
                nc.scalar.activation(cut(o_hi, c), cut(cv, c), ACT.Copy).then_inc(op_hi, 1)

            def result(name, norm, gain):
                def after(it, j):
                    act.wait_ge(evacuated, B0[name] + 4 * it + j + 1)
                    chunk(norm, 4 * it + j, j, gain)
                stage(name, None, after)

            result("pw2", "gu2", "ffn2_0")
            gate_up("gu2", 2, "gu2")
            down("dn2", "kv", "kv_norm")

            for m, m0 in ((1, 0), (2, 8)):
                for it in rounds(act, 2, peel=1 if m == 1 else 0):
                    for j in range(4):
                        split("kv", it + m0 // 4, 4, j + 2)
                        if m == 1 and isinstance(it, int) and it == 0 and j == 0:
                            root("kv")
                        act.wait_ge(evacuated, B0["kv"] + m0 + 4 * it + j + 1)
                        act.dma_start(qkv_dram[bass.ds(4 * it + j, 1), :, m, :].rearrange("c p n -> (c p) n"),
                                      (t0, t1)[j % 2][:]).then_inc(spilled[j % 2], 16)
            act.wait_ge(w_used, UEND["kv"])
            for c in range(KC):
                nc.scalar.activation(cut(h_hi, c), cut(x, c), ACT.Copy, scale=col("ffn1_1", c)).then_inc(op_hi, 1)
            gate_up("gu3", 3, None)
            down("dn3", "q", "mix_1")
            for it in rounds(act, 2, peel=1):
                for j in range(4):
                    split("q", it, 4, j + 2)
                    if isinstance(it, int) and it == 0 and j == 0:
                        root("q")
                    act.wait_ge(evacuated, B0["q"] + 4 * it + j + 1)
                    act.dma_start(qkv_dram[bass.ds(4 * it + j, 1), :, 0, :].rearrange("c p n -> (c p) n"),
                                  (t0, t1)[j % 2][:]).then_inc(spilled[j % 2], 16)

            sticks = [(half, kb) for half in range(2) for kb in reversed(range(TB))]
            for it in steps.loop(KC // 2, 16):
                for jj in range(2):
                    base = 16 * it + 8 * jj
                    act.wait_ge(s_v, 2 * it + jj + 1)
                    nc.scalar.activation(cut(v_st, jj), bank[5][:], ACT.Copy).then_inc(s_vout, 1)
                    for s in range(8 + 3):
                        if s < 8:
                            n = S - sticks[s][1] * P
                            e = s_e[:, (s % 2) * S:(s % 2) * S + n]
                            act.wait_ge(s_clip, base + s + 1)
                            steps.done(nc.scalar.activation(e, e, ACT.Exp))
                            nc.scalar.activation(e, e, ACT.Ln, bias=const("one")).then_inc(s_log, 1)
                        r = s - 3
                        if r >= 0:
                            n = S - sticks[r][1] * P
                            act.wait_ge(s_sum, base + r + 1)
                            if r >= 2:
                                act.wait_ge(s_pv, base + r - 1)
                            nc.scalar.activation(s_w[:, (r % 2) * S:(r % 2) * S + n], bank[r % 4][:, 0:n], ACT.Exp).then_inc(s_wt, 1)
                    act.wait_ge(s_pv, base + 8)
                    nc.scalar.activation(cut(o_hi, 2 * it + jj), bank[4][:], ACT.Copy).then_inc(op_hi, 1)
            result("o", "gu4", "ffn2_1")
            gate_up("gu4", 4, "gu4")
            down("dn4", "final", None)
            root("final")
            for c in range(KC):
                act.wait_ge(last_out, c + 1)
                act.dma_start(out[:, c * S:(c + 1) * S], cut(x, c)).then_inc(out_done, 16)
            act.wait_ge(out_done, 16 * KC)

        @block.vector
        def _(dve):
            steps = Steps(dve, dve_step)
            V = nc.vector

            def split(name, it, per, j):
                q, slot = U0[name] // RING + it * (per // RING) + j // RING, j % RING
                if isinstance(q, int) and 4 * q + slot >= UNITS:
                    return
                dve.wait_ge(w_hi_made, 4 * q + slot + 1)
                V.tensor_tensor(cut(w_lo, slot, UNIT), cut(w_raw, slot, UNIT), cut(w_hi, slot, UNIT).bitcast(f32), sub).then_inc(w_lo_made, 1)

            def lo_part(operand, c, gain, src=x, hi=h_hi, lo=h_lo, n=S):
                dve.wait_ge(op_hi, R0[operand] + c + 1)
                hi_c = cut(hi, c, n).bitcast(f32)
                if gain is None:
                    V.tensor_tensor(cut(lo, c, n), cut(src, c, n), hi_c, sub).then_inc(op_lo, 1)
                else:
                    V.scalar_tensor_tensor(cut(lo, c, n), cut(src, c, n), col(gain, c), hi_c, mult, sub).then_inc(op_lo, 1)

            def factor(name, dst=rB, n=S):
                dve.wait_ge(root_done, NORM[name] + 1)
                return V.reciprocal(dst[:, 0:n], dst[:, 0:n])

            def scaled(dst, src, r=None, by=None):
                r = rB[:] if r is None else r
                if by is None:
                    return V.tensor_tensor(dst, src, r, mult)
                return V.scalar_tensor_tensor(dst, src, by, r, mult, mult)

            def stage(name, norm, result, per=4, peel=0, count=0):
                n_it = (UEND[name] - U0[name]) // per
                peel = max(peel, 1 if norm else 0)
                if norm:
                    split(name, 0, per, 2)
                    steps.done(factor(norm))
                for it in steps.loop(n_it, count, peel):
                    for j in range(per):
                        if not (norm and isinstance(it, int) and it == 0 and j == 0):
                            split(name, it, per, j + 2)
                        dve.wait_ge(w_used, U0[name] + per * it + j + 1)
                        result(it, j)

            def gate_up(name, f, norm):
                def inner(it, j):
                    c = 2 * it + j // 2
                    b = B0[name] + 4 * it + j
                    if j % 2 and not (isinstance(c, int) and FC * f + c == 0):
                        dve.wait_ge(f_lo, FC * f + c)
                    scaled((t0, t1)[j % 2][:], bank[j][:]).then_inc(evacuated, 1)
                    if j % 2:
                        dve.wait_ge(acted, ACTED0[name] + c + 1)
                        dve.wait_ge(evacuated, b + 1)
                        V.tensor_tensor(t1[:], t0[:], t1[:], mult).then_inc(inner_made, 1)
                        dve.wait_ge(f_hi, FC * f + c + 1)
                        V.tensor_tensor(cut(a_lo, c), t1[:], cut(a_hi, c).bitcast(f32), sub).then_inc(f_lo, 1)
                stage(name, norm, inner)

            def down(name, operand, gain, by=0.5):
                def result(it, j):
                    if j % 3 == 2:
                        c = 4 * it + j // 3
                        V.scalar_tensor_tensor(cut(x, c), bank[j // 3][:], by, cut(x, c), mult, add).then_inc(evacuated, 1)
                        if gain is None:
                            return
                        lo_part(operand, c, gain)
                stage(name, None, result, per=12, peel=2 if name == "dn4" else 0)

            def post_chunk(c, yb, gain):
                dst = (t0, t1)[c % 2]
                steps.done(V.scalar_tensor_tensor(dst[:], cut(yb, c), col(gain, c), rB[:], mult, mult))
                V.tensor_tensor(cut(x, c), cut(x, c), dst[:], add).then_inc(posted, 1)

            def post(norm, yb, gain, operand, gain_next):
                steps.done(factor(norm))
                for c in range(KC + 1):
                    if c < KC:
                        post_chunk(c, yb, gain)
                    if c:
                        lo_part(operand, c - 1, gain_next)

            def backwards(half):
                return toep_st[:, half * S:(half + 1) * S][:, ::-1]

            def turn_in(i, par, dst, n):
                dve.wait_ge(v_turned, i + 1)
                V.tensor_copy(dst, bank[5 + par][:, 0:n].rearrange("p (b f) -> p b f", f=P)).then_inc(v_stored, 1)

            for j in range(2):
                split("in", 0, 4, j)
            V.memset(r_bias[:, 0:P], NEG).then_inc(bias_fill, 1)
            dve.wait_ge(loaded, 32)
            dve.wait_ge(x_in, 16)
            for c in range(KC):
                lo_part("mix", c, "mix_norm_pre")
            dve.wait_ge(bias_psum, 1)
            V.tensor_copy(r_bias[0:8, P:HBM_BIAS], bank[6][0:8, :]).then_inc(bias_sb, 1)
            V.memset(u_pad[:], 0.0).then_inc(pad_done, 1)
            V.memset(g_raw[:], 0.0).then_inc(pad_done, 1)

            split("in", 0, 4, 2)
            steps.done(factor("mix"))
            dve.wait_ge(pad_done, 2)
            idx = 0
            for b in range(22):
                if b:
                    split("in", 0, 4, b + 2)
                dve.wait_ge(w_used, b + 1)
                src = bank[b % 4][:]
                if b < 4:
                    scaled(cut(qT, b), src, by=DH ** -0.5).then_inc(evacuated, 1)
                elif b < 6:
                    w = b - 4
                    scaled(t0[:], src).then_inc(evacuated, 1)
                    dve.wait_ge(evacuated, b + 1)
                    if w:
                        dve.wait_ge(op_lo, R0["cmp"] + 1)
                    g = g_raw[:].rearrange("p (j n) -> p j n", n=GW)
                    for par in range(2):
                        for head in range(2):
                            s4 = t0[head * DH:(head + 1) * DH, :].rearrange("p (ch m e) -> p e m ch", e=2, m=8)[:, par]
                            for late in range(2):
                                V.tensor_copy(g[par * DH:(par + 1) * DH, 8 * late:8 * late + 8, head * NCMP:(head + 1) * NCMP],
                                              s4[:, :, late:late + NCMP]).then_inc(gather_part, 1)
                    V.tensor_copy(g[:, :, 2 * NCMP:2 * NCMP + 1],
                                  vec[:, VEC["pos_k"] + 16 * w:VEC["pos_k"] + 16 * w + 16].unsqueeze(2)).then_inc(gather_part, 1)
                    dve.wait_ge(gather_part, 9 * (w + 1))
                    dve.sem_inc(gathered, 1)
                    dve.wait_ge(op_hi, R0["cmp"] + w + 1)
                    V.tensor_tensor(g_lo[:, w * 16 * GW:(w + 1) * 16 * GW], g_raw[:],
                                    g_hi[:, w * 16 * GW:(w + 1) * 16 * GW].bitcast(f32), sub).then_inc(op_lo, 1)
                elif b < 8:
                    scaled((kS, kW)[b - 6][:], src).then_inc(evacuated, 1)
                elif b < 14:
                    if idx >= 2:
                        dve.wait_ge(v_turned, idx - 1)
                    scaled((t0, t1)[idx % 2][:], src).then_inc(evacuated, 1)
                    dve.wait_ge(evacuated, b + 1)
                    dve.sem_inc(v_ready, 1)
                elif b < 18:
                    c = b - 14
                    u = u_pad[:, c * (S + 3):(c + 1) * (S + 3)]
                    scaled(u[:, 3:], src).then_inc(evacuated, 1)
                    dve.wait_ge(evacuated, b + 1)
                    for k in range(4):
                        w = col("conv_w", 4 * c + k)
                        if k == 0:
                            last = V.tensor_scalar(cut(qk, c), u[:, 0:S], w, None, mult)
                        else:
                            last = V.scalar_tensor_tensor(cut(qk, c), u[:, k:k + S], w, cut(qk, c), mult, add)
                        if k < 3:
                            steps.done(last)
                    last.then_inc(conv_in, 1)
                else:
                    if b == 18:
                        dve.wait_ge(bias_out, 16)
                    scaled(cut(mo, b - 18), src).then_inc(evacuated, 1)
                if b - 2 in V_IN:
                    i = b - 2 - V_IN[0]
                    width, at = (2 * P, i * P) if i < 2 else (4 * P, (i - 2) * P)
                    tile = v_nsa if i < 2 else v_ml
                    turn_in(i, i % 2, tile[:].rearrange("p (b f) -> p b f", f=width)[:, :, at:at + P], S)
                if b in V_IN:
                    idx += 1
            split("in", 0, 4, 24)
            dve.wait_ge(w_used, 24)
            split("in", 0, 4, 25)
            for k in range(2):
                scaled(gsb[:, k * 256:(k + 1) * 256], bank[2][:, k * 256:(k + 1) * 256], rB[:, k * 256:(k + 1) * 256]).then_inc(evacuated, 1)
            dve.wait_ge(gates_turned, 1)
            V.tensor_copy(gate[:], bank[5][:, 0:TB * 24]).then_inc(gates_part, 1)
            dve.wait_ge(gates_part, 1)
            g0 = gate[:, 0:24].rearrange("p (h r) -> p h r", r=3)[:, :, 0]
            V.tensor_scalar(g0, g0, const("has_block"), None, mult).then_inc(gates_out, 1)

            def hidden_bias(w):
                for f in range(2):
                    V.tensor_copy(small[:, 2 * w + f:2 * w + f + 1], bank[2 * w + f][:, 2 * NCMP:2 * NCMP + 1]).then_inc(hid_bias, 1)

            for u in range(8):
                if u < 6:
                    split("cmp", 0, 4, u + 2)
                if u == 3 or u == 7:
                    dve.wait_ge(w_used, U0["cmp"] + u + 1)
                    hidden_bias(u // 4)
            dve.wait_ge(cmp_proj, 1)
            V.tensor_copy(kc[:, 0:NCMP], bank[4][:, 0:NCMP]).then_inc(cmp_out, 1)
            V.tensor_copy(vc[0:NCMP, :], bank[5][0:NCMP, 0:P]).then_inc(cmp_out, 1)
            for u in (6, 7):
                split("cmp", 0, 4, u + 2)

            dve.wait_ge(toep_in, 16)
            items = [(half, qb, br) for half in range(2) for qb in range(TB) for br in range(3)]
            NI = len(items)
            for c in steps.loop(4, 4 + NI):
                V.tensor_copy(q_st[:], cut(qT, c)).then_inc(n_q, 1)
                last = None
                for half in range(2):
                    steps.done(V.tensor_copy(backwards(half), cut(toep, c + 4 * half)))
                    src = gate[:].rearrange("p (q h n) -> p q h n", h=2, n=12)[:, :, half, bass.ds(3 * c, 3)]
                    steps.done(V.tensor_copy(gate_st[:, half * 12:(half + 1) * 12].rearrange("p (q r) -> p q r", r=3), src))
                for s in range(NI + 1):
                    if s < NI:
                        half, qb, br = items[s]
                        n = (8 * qb + 7) if br == 0 else P * (qb + 1)
                        dve.wait_ge(n_qk, NI * c + s + 1)
                        if s >= 2:
                            dve.wait_ge(n_exp, NI * c + s - 1)
                        dve.sem_inc(n_seen, 1)
                        at = half * S
                        bias = (toep_st[:, at + 31 + P * (3 - qb):at + S:16] if br == 0 else toep_st[:, at + S - n:at + S])
                        V.tensor_tensor_reduce(s_sb[:, (s % 2) * S:(s % 2) * S + n], bank[s % 2][:, 0:n], bias, -1.0, 3.0e38,
                                               add, amin, small[:, 8 + s % 2:9 + s % 2]).then_inc(n_add, 1)
                    r = s - 1
                    if r >= 0:
                        half, qb, br = items[r]
                        n = (8 * qb + 7) if br == 0 else P * (qb + 1)
                        dve.wait_ge(n_exp, NI * c + r + 1)
                        inv = small[:, 16 + r % 2:17 + r % 2]
                        steps.done(V.reciprocal(inv, small[:, 12 + r % 2:13 + r % 2]))
                        pr = p_sb[:, (r % 3) * S:(r % 3) * S + n]
                        g = half * 12 + qb * 3 + br
                        V.tensor_scalar(pr, pr, inv, gate_st[:, g:g + 1], mult, mult).then_inc(n_scaled, 1)
                dve.wait_ge(op_hi, R0["nsa"] + c + 1)
                V.tensor_tensor(cut(h_lo, c), bank[4][:], cut(h_hi, c).bitcast(f32), sub).then_inc(op_lo, 1)

            dve.wait_ge(gb_in, 16)
            row = lambda k: rows[0:4, k * S:(k + 1) * S]
            bi, bf = gbias[0:4, 0:1], gbias[0:4, 1:2]
            steps.done(V.tensor_copy(row(0), gsb[MI:MI + 4, :]))
            steps.done(V.tensor_copy(row(1), gsb[MF:MF + 4, :]))
            steps.done(V.tensor_scalar(row(0), row(0), bi, None, add))
            steps.done(V.tensor_scalar(row(1), row(1), bf, None, add))
            V.scalar_tensor_tensor(row(4), row(1), -1.0, row(1), mult, amax).then_inc(m_abs, 1)
            V.memset(row(5), 0.0).then_inc(m_abs, 1)
            dve.wait_ge(m_soft, 1)
            dve.wait_ge(m_abs, 2)
            steps.done(V.scalar_tensor_tensor(row(1), row(1), 0.0, row(4), amin, sub))
            steps.done(V.tensor_tensor_scan(row(2), row(1), row(5), 0.0, add, amin))
            steps.done(V.tensor_copy(row(1), row(2)))
            steps.done(V.tensor_tensor(row(0), row(0), row(1), sub))
            steps.done(V.tensor_tensor_scan(row(2), row(0), row(0), 0.0, amax, amax))
            steps.done(V.scalar_tensor_tensor(row(3), row(1), -1.0, row(2), mult, sub))
            V.tensor_scalar(row(2), row(2), -1.0, None, mult).then_inc(m_row, 1)
            dve.wait_ge(m_col, 1)
            V.tensor_copy(a_col[:], bank[2][:, 0:16]).then_inc(m_colout, 1)
            dve.wait_ge(m_colout, 1)
            for i in range(16):
                hd, kb = divmod(i, TB)
                dve.wait_ge(m_bc, hd + 1)
                if i >= 2:
                    dve.wait_ge(m_decay, i - 1)
                V.scalar_tensor_tensor(diag[:, (i % 2) * P:(i % 2 + 1) * P], bank[0][:, kb * P:(kb + 1) * P],
                                       a_col[:, 4 * kb + hd:4 * kb + hd + 1], const("not_after"), add, add).then_inc(m_diag, 1)
                n = S - kb * P
                dve.wait_ge(m_qk, i + 1)
                dve.wait_ge(m_decay, i + 1)
                if i >= 2:
                    dve.wait_ge(m_pv, i - 1)
                V.scalar_tensor_tensor(weight[:, (i % 2) * S:(i % 2) * S + n], bank[2 + i % 2][:, 0:n], DH ** -0.5,
                                       decay[:, (i % 2) * S:(i % 2) * S + n], mult, mult).then_inc(m_weight, 1)
                if kb == 3:
                    dve.wait_ge(m_pv, 4 * hd + 4)
                    dve.wait_ge(m_floor, hd + 1)
                    steps.done(V.scalar_tensor_tensor(t0[:], bank[6 + hd % 2][:], -1.0, floor[:], mult, amax))
                    steps.done(V.tensor_tensor(t0[:], bank[6 + hd % 2][:], t0[:], amax))
                    steps.done(V.reciprocal(t0[:], t0[:]))
                    V.tensor_tensor(cut(h_ml, hd), bank[4 + hd % 2][:], t0[:], mult).then_inc(m_h, 1)
            dve.wait_ge(acted_mix, 8)
            for hd in range(4):
                dve.wait_ge(m_root, hd + 1)
                steps.done(V.reciprocal(cut(rows, hd), cut(rows, hd)))
                steps.done(V.scalar_tensor_tensor(cut(h_ml, hd), cut(h_ml, hd), col("mlstm_norm", hd), cut(rows, hd), mult, mult))
                V.tensor_tensor(cut(h_ml, hd), cut(h_ml, hd), cut(mo, hd), mult).then_inc(m_out, 1)
                dve.wait_ge(op_hi, R0["ml"] + hd + 1)
                V.tensor_tensor(cut(h_lo, 4 + hd), cut(h_ml, hd), cut(h_hi, 4 + hd).bitcast(f32), sub).then_inc(op_lo, 1)
            dve.wait_ge(mem_in, 16)
            for c in range(KC):
                lo_part("mem", c, "mem_norm", mem, m_hi, m_lo, MEM)

            for u in range(8):
                split("out", 0, 4, u + 2)
                if u == 1:
                    factor("mem", rM, MEM).then_inc(r_done, 1)
                dve.wait_ge(w_used, U0["out"] + u + 1)
                V.tensor_copy(cut(yb_x, u), bank[u % 4][:]).then_inc(evacuated, 1)
            split("xkv", 0, 4, 2)
            steps.done(factor("post_mix"))
            dve.wait_ge(r_done, 1)
            for u in range(8):
                if u:
                    split("xkv", 0, 4, u + 2)
                post_chunk(u, yb_x, "mix_norm_post")
                dve.wait_ge(w_used, U0["xkv"] + u + 1)
                scaled(cut(kx, u, MEM), bank[u % 4][:, 0:MEM], rM[:]).then_inc(evacuated, 1)
                lo_part("xq", u, "xattn_norm_pre")
            vx3 = vx[:].rearrange("p (b f) -> p b f", f=D)
            for it in rounds(dve, 2):
                for j in range(4):
                    split("xkv", it + 2, 4, j + 2)
                    dve.wait_ge(w_used, U0["xkv"] + 8 + 4 * it + j + 1)
                    i = 6 + 4 * it + j
                    if j >= 2:
                        dve.wait_ge(v_turned, i - 1)
                    scaled((t0, t1)[j % 2][:, 0:MEM], bank[j][:, 0:MEM], rM[:]).then_inc(evacuated, 1)
                    dve.wait_ge(evacuated, B0["xkv"] + 8 + 4 * it + j + 1)
                    dve.sem_inc(v_ready, 1)
                    if j:
                        turn_in(i - 1, (j - 1) % 2, vx3[:, :, bass.ds((4 * it + j - 1) * P, P)], MEM)
                turn_in(6 + 4 * it + 3, 1, vx3[:, :, bass.ds((4 * it + 3) * P, P)], MEM)

            def xq_out(it, j):
                scaled(cut(qx, 4 * it + j), bank[j][:], by=256 ** -0.5).then_inc(evacuated, 1)
            stage("xq", "xq", xq_out)
            for s in range(16 + 1):
                if s < 16:
                    dve.wait_ge(x_qk, s + 1)
                    V.tensor_reduce(small[:, 8 + s % 2:9 + s % 2], bank[s % 2][:, 0:MEM], AX.X, amax, negate=True).then_inc(x_max, 1)
                r = s - 1
                if r >= 0:
                    dve.wait_ge(x_exp, r + 1)
                    inv = small[:, 16 + r % 2:17 + r % 2]
                    steps.done(V.reciprocal(inv, small[:, 12 + r % 2:13 + r % 2]))
                    V.tensor_scalar(cut(px, r % 3, MEM), cut(px, r % 3, MEM), inv, None, mult).then_inc(x_scaled, 1)
                if s >= 6 and s % 4 == 2 or s == 16:
                    heads = [(s - 6) // 4] if s < 16 else [3]
                    for hd in heads:
                        for dv in range(2):
                            c = 2 * hd + dv
                            dve.wait_ge(op_hi, R0["xo"] + c + 1)
                            V.tensor_tensor(cut(h_lo, c), bank[4 + dv][:], cut(h_hi, c).bitcast(f32), sub).then_inc(op_lo, 1)

            def xo_out(it, j):
                V.tensor_copy(cut(yb_x, 4 * it + j), bank[j][:]).then_inc(evacuated, 1)
            stage("xo", None, xo_out)
            post("post_x", yb_x, "xattn_norm_post", "gu0", "ffn_norm_pre")
            gate_up("gu0", 0, "gu0")

            def dn0_out(it, j):
                if j % 3 == 2:
                    V.tensor_copy(cut(yb_h, 4 * it + j // 3), bank[j // 3][:]).then_inc(evacuated, 1)
            stage("dn0", None, dn0_out, per=12)
            post("post_ffn", yb_h, "ffn_norm_post", "gu1", "ffn1_0")
            gate_up("gu1", 1, "gu1")
            down("dn1", "pw1", "mix_0")
            V.memset(u_conv[:], 0.0).then_inc(pad_done, 1)
            dve.wait_ge(pad_done, 3)

            def glu(it, j):
                scaled((t1, t0)[j % 2][:], bank[j][:]).then_inc(evacuated, 1)
                if j % 2:
                    c = 2 * it + j // 2
                    dve.wait_ge(acted, ACTED0["pw1"] + c + 1)
                    at = c * (S + PAD)
                    steps.done(V.scalar_tensor_tensor(u_conv[:, bass.ds(at + PAD, S)], t1[:], col("b_pw1", c), t0[:], add, mult))
                    for k in range(TAPS):
                        u, w = u_conv[:, bass.ds(at + k, S)], col("w_dw", c * TAPS + k)
                        if k == 0:
                            steps.done(V.tensor_scalar(cut(cv, c), u, w, col("b_dw", c), mult, add))
                        elif k < TAPS - 1:
                            steps.done(V.scalar_tensor_tensor(cut(cv, c), u, w, cut(cv, c), mult, add))
                        else:
                            V.scalar_tensor_tensor(cut(cv, c), u, w, cut(cv, c), mult, add).then_inc(c_conv, 1)
            stage("pw1", "pw1", glu, count=2 * TAPS)
            dve.wait_ge(root_done, NORM["ln_mean"] + 1)
            dve.wait_ge(c_conv, KC)
            for c in range(KC):
                V.tensor_tensor(cut(cv, c), cut(cv, c), rB[:], sub).then_inc(c_cent, 1)
            steps.done(factor("ln_var"))
            for c in range(KC + 1):
                if c < KC:
                    V.tensor_tensor(cut(cv, c), cut(cv, c), rB[:], mult).then_inc(c_norm, 1)
                if c:
                    lo_part("pw2", c - 1, None, cv, o_hi, o_lo)

            def result(name, operand, gain, bias):
                def after(it, j):
                    c = 4 * it + j
                    V.scalar_tensor_tensor(cut(x, c), bank[j][:], 0.0 if bias is None else col(bias, c), cut(x, c), add, add).then_inc(evacuated, 1)
                    lo_part(operand, c, gain)
                stage(name, None, after)

            result("pw2", "gu2", "ffn2_0", "b_pw2")
            gate_up("gu2", 2, "gu2")
            down("dn2", "kv", "kv_norm")

            def spill(n0, per_round, by=None):
                def after(it, j):
                    n = n0 + per_round * it + j
                    if not (isinstance(it, int) and n < 2):
                        dve.wait_ge(spilled[j % 2], 8 * (n - j % 2))
                    scaled((t0, t1)[j % 2][:], bank[j][:], by=by).then_inc(evacuated, 1)
                return after
            stage("kv", "kv", spill(0, 4))
            for c in range(KC):
                lo_part("gu3", c, "ffn1_1")
            for par in range(2):
                dve.wait_ge(spilled[par], 16 * 8)
            gate_up("gu3", 3, None)
            down("dn3", "q", "mix_1")
            stage("q", "q", spill(16, 4, DH ** -0.5))

            sticks = [(half, kb) for half in range(2) for kb in reversed(range(TB))]
            for it in rounds(dve, KC // 2):
                for jj in range(2):
                    base = 16 * it + 8 * jj
                    for s in range(8 + 1):
                        if s < 8:
                            n = S - sticks[s][1] * P
                            dve.wait_ge(s_qk, base + s + 1)
                            if s >= 2:
                                dve.wait_ge(s_soft, base + s - 1)
                            V.tensor_scalar(s_e[:, (s % 2) * S:(s % 2) * S + n], bank[s % 4][:, 0:n], 40.0, None, amin).then_inc(s_clip, 1)
                        r = s - 1
                        if r >= 0:
                            half, kb = sticks[r]
                            n = S - kb * P
                            dve.wait_ge(s_log, base + r + 1)
                            V.tensor_tensor(s_l[:, (half * TB + kb) * S:(half * TB + kb) * S + n], bank[r % 4][:, 0:n],
                                            s_e[:, (r % 2) * S:(r % 2) * S + n], amax).then_inc(s_soft, 1)
                    dve.wait_ge(s_soft, base + 8)
                    dve.wait_ge(op_hi, R0["o"] + 2 * it + jj + 1)
                    V.tensor_tensor(cut(o_lo, 2 * it + jj), bank[4][:], cut(o_hi, 2 * it + jj).bitcast(f32), sub).then_inc(op_lo, 1)
            result("o", "gu4", "ffn2_1", None)
            gate_up("gu4", 4, "gu4")
            down("dn4", "final", None)
            steps.done(factor("final"))
            for c in range(KC):
                V.scalar_tensor_tensor(cut(x, c), cut(x, c), col("final_norm", c), rB[:], mult, mult).then_inc(last_out, 1)

        @block.gpsimd
        def _(pool):
            G = nc.gpsimd
            pool.dma_start(onehot[0:32, 0:S + 8], t["onehot_rel"]).then_inc(rel_in, 16)
            pool.dma_start(cmp_w2[:], t["cmp_w2"]).then_inc(w2_in, 16)
            pool.dma_start(gbias[0:4, :], t["gate_bias"]).then_inc(gb_in, 16)

            def sum_chunks(name, n=S, src=None):
                base = 9 * NORM[name]
                if NORM[name]:
                    pool.wait_ge(stat_done, NORM[name])
                G.memset(acc[:, 0:n], 0.0).then_inc(summed, 1)
                for c in range(KC):
                    if src is None:
                        pool.wait_ge(squared, SQ0[name] + c + 1)
                        add_in = sq[:, (c % 2) * S:(c % 2) * S + n]
                    else:
                        pool.wait_ge(c_conv, c + 1)
                        add_in = cut(src, c)
                    pool.wait_ge(summed, base + c + 1)
                    G.tensor_tensor(acc[:, 0:n], acc[:, 0:n], add_in, add).then_inc(summed, 1)

            sum_chunks("mix")
            pool.wait_ge(bias_sb, 1)
            pool.wait_ge(bias_fill, 1)
            pool.dma_start(bias_dram, r_bias[0:8, :]).then_inc(bias_out, 16)
            pool.wait_ge(bias_out, 16)
            pool.dma_start(toep[:].rearrange("p (h n) -> p h n", n=S),
                           bass.AP(tensor=bias_dram.tensor, offset=1, ap=[[1, P], [HBM_BIAS, 8], [1, S]])).then_inc(toep_in, 16)
            pool.wait_ge(op_lo, R0["ml"] + 4)
            pool.dma_start(mem[:], t["mem"].rearrange("p c n -> p (c n)")).then_inc(mem_in, 16)
            sum_chunks("mem", MEM)
            sum_chunks("post_mix")
            sum_chunks("xq")
            sum_chunks("post_x")
            sum_chunks("gu0")
            sum_chunks("post_ffn")
            sum_chunks("gu1")
            sum_chunks("pw1")
            sum_chunks("ln_mean", src=cv)
            sum_chunks("ln_var")
            sum_chunks("gu2")
            sum_chunks("kv")
            sum_chunks("q")
            sum_chunks("gu4")
            sum_chunks("final")


_VECTORS = {
    "mix_norm_pre": "mix_norm_pre", "mix_norm_post": "mix_norm_post", "xattn_norm_pre": "xattn_norm_pre",
    "mem_norm": "mem_norm", "xattn_norm_post": "xattn_norm_post", "ffn_norm_pre": "ffn_norm_pre",
    "ffn_norm_post": "ffn_norm_post", "kv_norm": "kv_norm_2", "final_norm": "final_norm_2", "b_dw": "conv_b_dw_2",
    "ln_g": "conv_ln_g_2", "ln_b": "conv_ln_b_2", "b_pw2": "conv_b_pw2_2", "conv_b": "conv_b", "mlstm_norm": "mlstm_norm",
}


def columns(v):
    return v.reshape(-1, P).T


def weight_blocks(w):
    k, n = w.shape
    return np.ascontiguousarray(w.reshape(k // P, P, n // P, P).transpose(2, 1, 0, 3))


def interleave(a, b):
    k, n = a.shape
    return np.stack([a.reshape(k, n // P, P), b.reshape(k, n // P, P)], axis=2).reshape(k, 2 * n)


def buckets_by_distance():
    n = np.arange(S)
    exact = 16
    large = exact + (np.log(np.maximum(n, 1).astype(np.float32) / np.float32(exact))
                     / np.float32(np.log(128 / exact)) * np.float32(32 - exact)).astype(np.int32)
    bucket = np.where(n < exact, n, np.minimum(large, 31))
    return (np.arange(32)[:, None] == bucket[None, :]).astype(np.float32)


def constants():
    r = np.arange(P)
    one = np.ones((P, P), np.float32)
    made = {
        "ident": np.eye(P, dtype=np.float32), "ones": one, "minus_ones": -one,
        "mask_from_query": (r[None, :] >= r[:, None]) * np.float32(-1e30),
        "minus_from_here": -(r[:, None] >= r[None, :]).astype(np.float32),
        "not_after": np.where(r[:, None] > r[None, :], np.float32(NEG), np.float32(0)),
        "pick": np.repeat((r[:, None] == np.arange(4)[None, :]).astype(np.float32), P, axis=1),
        "has_block": (r[:, None] >= 31).astype(np.float32), "one": one[:, :1],
        "norm_eps": one[:, :1] * np.float32(1e-6), "ln_eps": one[:, :1] * np.float32(1e-5),
    }
    return np.ascontiguousarray(np.concatenate([made[n] for n, _ in CONSTS], axis=1), dtype=np.float32)


def lay_out(a):
    vec = {n: columns(a[src].reshape(-1)) for n, src in _VECTORS.items()}
    for i in range(2):
        vec[f"ffn1_{i}"], vec[f"mix_{i}"] = columns(a["ffn1_norm_2"][i]), columns(a["mix_norm_2"][i])
        vec[f"ffn2_{i}"] = columns(a["ffn2_norm_2"][i])
    vec["b_pw1"] = columns(a["conv_b_pw1_2"][0])
    vec["w_dw"] = a["conv_w_dw_2"][0].reshape(TAPS, KC, P).transpose(2, 1, 0).reshape(P, -1)
    vec["conv_w"] = a["conv_w"][0].reshape(4, 4, P).transpose(2, 1, 0).reshape(P, -1)
    for n in "kv":
        vec[f"pos_{n}"] = a[f"cmp_pos_{n}"][0].reshape(16, P).T
    w = a["w_in"][0]
    parts = np.split(w, np.cumsum([512] + [128] * 6 + [24, 256, 256, 512, 4, 4]), axis=1)
    nq, kc, vc, ks, vs, kw, vw, gt, mq, mk, mv, mi, mf, mo = parts
    heads = [h for c in range(4) for h in (c, c + 4)]
    nq = nq.reshape(D, 8, DH)[:, heads].reshape(D, 512)
    w_in = np.concatenate([nq, kc, vc, ks, kw, vs, vw, mv, mq, mk, mo], axis=1)
    gates = np.zeros((D, P), np.float32)
    gates[:, GT:GT + 24], gates[:, MI:MI + 4], gates[:, MF:MF + 4] = gt, mi, mf
    w_out = a["w_out"][0]
    w_out = np.concatenate([w_out[:512].reshape(8, DH, D)[heads].reshape(512, D), w_out[512:]], axis=0)
    half = lambda m: np.split(m, 2, axis=1)
    laid = {
        "vectors": np.ascontiguousarray(np.concatenate([vec[n] for n, _ in VECTORS], axis=1)),
        "consts": constants(),
        "x": np.ascontiguousarray(a["x"][0].T.reshape(KC, P, S).transpose(1, 0, 2)),
        "mem": np.ascontiguousarray(a["mem"][0].T.reshape(KC, P, MEM).transpose(1, 0, 2)),
        "onehot_rel": np.ascontiguousarray(np.concatenate([buckets_by_distance(), a["rel_bias"].T], axis=1)),
        "cmp_w2": np.ascontiguousarray(np.stack([a["cmp_w2_k"][0].reshape(2, P, DH), a["cmp_w2_v"][0].reshape(2, P, DH)])
                                       .transpose(2, 0, 1, 3).reshape(P, -1)),
        "gate_bias": np.ascontiguousarray(a["mlstm_gate_bias"][0].T),
        "w_in": weight_blocks(w_in), "w_gates": weight_blocks(gates)[0],
        "cmp_w1": np.ascontiguousarray(np.concatenate([a["cmp_w1_k"][0], a["cmp_w1_v"][0]])
                                       .reshape(8, 4, P, 2 * P).transpose(0, 2, 1, 3)),
        "w_out": weight_blocks(w_out), "w_xkv": weight_blocks(a["w_xkv"][0]), "w_xq": weight_blocks(a["w_xq"][0]),
        "w_xo": weight_blocks(a["w_xo"][0]),
        "w_gu0": weight_blocks(interleave(*half(a["w_gate_up"][0]))), "w_dn0": weight_blocks(a["w_down"][0]),
        "w_pw1": weight_blocks(interleave(*half(a["conv_w_pw1_2"][0]))), "w_pw2": weight_blocks(a["conv_w_pw2_2"][0]),
        "w_kv": weight_blocks(a["w_kv_2"]), "w_q": weight_blocks(a["attn_w_q_2"][0]), "w_o": weight_blocks(a["attn_w_o_2"][0]),
    }
    for n, (ffn, layer) in enumerate([("ffn1", 0), ("ffn2", 0), ("ffn1", 1), ("ffn2", 1)], start=1):
        laid[f"w_gu{n}"] = weight_blocks(interleave(a[f"{ffn}_w_gate_2"][layer], a[f"{ffn}_w_up_2"][layer]))
        laid[f"w_dn{n}"] = weight_blocks(a[f"{ffn}_w_down_2"][layer])
    return laid


def kernel(**inputs):
    import concourse.bacc as bacc
    from concourse.bass_utils import run_bass_kernel_spmd as run

    nc = bacc.Bacc("TRN2", target_bir_lowering=False, num_devices=1)
    laid = lay_out({n: np.asarray(v) for n, v in inputs.items()})
    t = {n: nc.dram_tensor("in_" + n, v.shape, mybir.dt.from_np(v.dtype), kind="ExternalInput").ap() for n, v in laid.items()}
    out = nc.dram_tensor("out", (P, KC * S), mybir.dt.float32, kind="ExternalOutput").ap()
    block_program(nc, t, out)
    got = run(nc, [{"in_" + n: v for n, v in laid.items()}], core_ids=[0]).results[0]["out"]
    return np.ascontiguousarray(got.reshape(P, KC, S).transpose(2, 1, 0).reshape(1, S, D))
```

```python
import concourse.bass as bass
import numpy as np
from concourse import mybir
from contextlib import ExitStack

P = 128
D, S, MEM, DFF = 1024, 512, 256, 2816
KC = D // P
FC = DFF // P
TB = S // P
DH = 64
NCMP = S // 16 - 1
GW = 2 * NCMP + 2
TAPS = 31
PAD = TAPS - 1
TAPS_PE, TAPS_POOL = 8, 7
TAPS_DVE = TAPS - TAPS_PE - TAPS_POOL
NSA_ITEMS = [(half, qb, br) for half in range(2) for qb in range(TB) for br in range(3)]
FACTOR_BANK = [5, 6, 7, 4]
NEG = -1.0e30
STICKS = {0: (0, S), 1: (S, S - P), 3: (2 * S - P, P), 2: (2 * S, S - 2 * P)}
STICK = 2 * S + S // 2
UNIT = KC * P
RING = 4
DN_KS = [(0, 8), (8, 8), (16, 6)]
GT, MI, MF = 0, 32, 64
HBM_BIAS = P + S

STAGES = [("in", 24, 24), ("cmp", 8, 0), ("out", 8, 8), ("xkv", 16, 16), ("xq", 8, 8), ("xo", 8, 8),
          ("gu0", 44, 44), ("dn0", 24, 8), ("gu1", 44, 44), ("dn1", 24, 8), ("pw1", 16, 16),
          ("pw2", 8, 8), ("gu2", 44, 44), ("dn2", 24, 8), ("kv", 16, 16), ("gu3", 44, 44),
          ("dn3", 24, 8), ("q", 8, 8), ("o", 8, 8), ("gu4", 44, 44), ("dn4", 24, 8)]
OPERANDS = [("mix", 8), ("cmp", 2), ("nsa", 4), ("ml", 4), ("mem", 8), ("xq", 8), ("xo", 8),
            ("gu0", 8), ("gu1", 8), ("pw1", 8), ("pw2", 8), ("gu2", 8), ("kv", 8), ("gu3", 8),
            ("q", 8), ("o", 8), ("gu4", 8)]
NORMS = [("mix", 1), ("mem", 1), ("post_mix", 1), ("xq", 1), ("post_x", 1), ("gu0", 1),
         ("post_ffn", 1), ("gu1", 1), ("pw1", 1), ("ln_mean", 0), ("ln_var", 1), ("gu2", 1),
         ("kv", 1), ("q", 1), ("gu4", 1), ("final", 1)]
VECTORS = [("mix_norm_pre", 8), ("mix_norm_post", 8), ("xattn_norm_pre", 8), ("mem_norm", 8),
           ("xattn_norm_post", 8), ("ffn_norm_pre", 8), ("ffn_norm_post", 8), ("ffn1_0", 8),
           ("ffn1_1", 8), ("mix_0", 8), ("mix_1", 8), ("ffn2_0", 8), ("ffn2_1", 8), ("kv_norm", 8),
           ("final_norm", 8), ("b_pw1", 16), ("b_dw", 8), ("ln_g", 8), ("ln_b", 8), ("b_pw2", 8),
           ("w_dw", 8 * TAPS), ("conv_w", 16), ("conv_b", 4), ("mlstm_norm", 4), ("pos_k", 16),
           ("pos_v", 16)]
CONSTS = [("ident", P), ("ones", P), ("minus_ones", P), ("mask_from_query", P), ("minus_from_here", P), ("not_after", P),
          ("pick", 4 * P), ("to_row", 16), ("has_block", 1), ("one", 1), ("zero", 1), ("norm_eps", 1), ("ln_eps", 1)]


def starts(sizes):
    found, at = {}, 0
    for name, size, *_ in sizes:
        found[name], at = at, at + size
    return found, at


U0, UNITS = starts(STAGES)
B0, _ = starts([(n, b) for n, _, b in STAGES])
UEND = {n: U0[n] + k for n, k, _ in STAGES}
BEND = {n: B0[n] + b for n, _, b in STAGES}
R0, _ = starts(OPERANDS)
SQ0, _ = starts([(n, 8 * sq) for n, sq in NORMS])
ACTED0, _ = starts([("gu0", FC), ("gu1", FC), ("pw1", KC), ("gu2", FC), ("gu3", FC), ("gu4", FC)])
SUM0, _ = starts([(n, 9 * sq) for n, sq in NORMS])
NORM = {n: i for i, (n, _) in enumerate(NORMS)}
VEC, NVEC = starts(VECTORS)
CST, NCST = starts(CONSTS)


def rounds(eng, n, peel=0):
    for i in range(min(peel, n)):
        yield i
    if n > peel:
        with eng.Fori(peel, n) as i:
            yield i


class Steps:

    def __init__(self, eng, sem):
        self.eng, self.sem, self.base, self.n = eng, sem, 0, 0

    def done(self, instruction):
        self.eng.wait_ge(self.sem, self.mark(instruction))

    def mark(self, instruction):
        instruction.then_inc(self.sem, 1)
        self.n += 1
        return self.base + self.n

    def loop(self, n, per, peel=0):
        first = self.base + self.n
        for i in rounds(self.eng, n, peel):
            self.base, self.n = first + i * per, 0
            yield i
            assert self.n == per, (self.n, per)
        self.base, self.n = first + n * per, 0


def block_program(nc, t, out):
    f32, f32r = mybir.dt.float32, mybir.dt.float32r
    ALU, ACT, AX = mybir.AluOpType, mybir.ActivationFunctionType, mybir.AxisListType
    mult, add, sub, amax, amin = ALU.mult, ALU.add, ALU.subtract, ALU.max, ALU.min
    ctx = ExitStack()
    with ctx:
        def held(stack):
            return lambda name, width, dt=f32: stack.enter_context(nc.sbuf_tensor(name, [P, width], dt))

        sb = held(ctx)

        def sem(name):
            return ctx.enter_context(nc.semaphore(name))

        def dram(name, shape):
            return nc.dram_tensor(name, shape, f32).ap()

        w_raw, w_hi, w_lo = sb("w_raw", RING * UNIT), sb("w_hi", RING * UNIT, f32r), sb("w_lo", RING * UNIT, f32r)
        x = sb("x", KC * S)
        vec, cst = sb("vec", NVEC), sb("cst", NCST)
        rB = sb("rB", S)
        sq, acc = sb("sq", 2 * S), sb("acc", S)
        t0, t1 = sb("t0", S), sb("t1", S)
        small = sb("small", 64)
        with ExitStack() as h:
            yb_h = held(h)("yb_h", KC * S)
        h_hi, h_lo = sb("h_hi", KC * S, f32r), sb("h_lo", KC * S, f32r)
        with ExitStack() as ph:
            a_hi, a_lo = held(ph)("a_hi", FC * S, f32r), held(ph)("a_lo", FC * S, f32r)
        with ExitStack() as ph:
            p = held(ph)
            qT, kS, kW = p("qT", 4 * S), p("kS", S), p("kW", S)
            v_nsa = p("v_nsa", TB * 2 * P)
            v_ml = p("v_ml", TB * 4 * P)
            qk, mo, gsb = p("qk", 4 * S), p("mo", 4 * S), p("gsb", S)
            gate, kc, vc = p("gate", TB * 24), p("k_cmp", NCMP + 1), p("v_cmp", P)
            cmp_h, cmp_w2, gbias = p("cmp_h", 4 * GW), p("cmp_w2", 4 * DH), p("gbias", 2)
            with ExitStack() as q:
                p2 = held(q)
                toep = p2("toep", 8 * S)
                with ExitStack() as r:
                    p3 = held(r)
                    u_pad, g_raw = p3("u_pad", 4 * (S + 3)), p3("g_raw", 16 * GW)
                    g_hl = p3("g_hl", 2 * 16 * 2 * GW, f32r)
                    g_parts = g_hl[:].rearrange("p (w j t n) -> p w j t n", w=2, t=2, n=GW)
                onehot, r_bias = qk[:, 0:S + 8], mo[:, 0:HBM_BIAS]
                with ExitStack() as r:
                    p3 = held(r)
                    q_st, s_sb, p_sb, pT = p3("q_st", S), p3("s_sb", 2 * S), p3("p_sb", 3 * S), p3("pT", 2 * S)
                    toep_st, gate_st = p3("toep_st", 2 * S), p3("gate_st", 2 * TB * 3)
            with ExitStack() as q:
                p2 = held(q)
                rows = p2("rows", 5 * S)
                a_col, decay, weight = p2("a_col", TB * 4), p2("decay", 2 * S), p2("weight", 2 * S)
                diag, floor, h_ml = p2("diag", 2 * P), p2("floor", S), p2("h_ml", 4 * S)
        with ExitStack() as ph:
            p = held(ph)
            yb_x, mem, rM = p("yb_x", KC * S), p("mem", KC * MEM), p("rM", MEM)
            m_hi, m_lo = p("m_hi", KC * MEM, f32r), p("m_lo", KC * MEM, f32r)
            kx, vx, qx = p("kx", KC * MEM), p("vx", 2 * D), p("qx", KC * S)
            px, pxT = p("px", 3 * MEM), p("pxT", 2 * 2 * S)
        with ExitStack() as ph:
            p = held(ph)
            o_hi, o_lo = p("o_hi", KC * S, f32r), p("o_lo", KC * S, f32r)
            with ExitStack() as q:
                p2 = held(q)
                u_conv, cv = p2("u_conv", KC * (S + PAD)), p2("cv", KC * S)
                diag_w, c_acc = p2("diag_w", 2 * TAPS_PE * P), p2("c_acc", 2 * S)
                c_product = p2("c_product", 2 * S)
            with ExitStack() as q:
                p2 = held(q)
                qkv, v_st = p2("qkv", 2 * 3 * S), p2("v_st", 2 * S)
                s_l, s_w = p2("s_l", 2 * STICK), p2("s_w", 2 * STICK)
                s_later = p2("s_later", 2 * 3 * P)
                ident_b, mask_b = held(q)("ident_b", P, mybir.dt.bfloat16), held(q)("mask_b", P, mybir.dt.bfloat16)
        banks = [ctx.enter_context(nc.psum_tensor(f"bank{i}", [P, 4 * S], f32)) for i in range(2)]
        bank = [banks[i // 4][:, (i % 4) * S:(i % 4 + 1) * S] for i in range(8)]
        bias_dram, qkv_dram = dram("bias_by_distance", (8, HBM_BIAS)), dram("stick_qkv", (KC, P, 3, S))

        raw_in = [sem(f"raw_in{i}") for i in range(RING)]
        w_hi_made, w_lo_made = sem("w_hi_made"), sem("w_lo_made")
        w_used = sem("w_used")
        evacuated = sem("evacuated")
        op_hi, op_lo = sem("op_hi"), sem("op_lo")
        f_hi, f_lo = sem("f_hi"), sem("f_lo")
        squared, summed = sem("squared"), sem("summed")
        stat_done, root_done, r_done = sem("stat_done"), sem("root_done"), sem("r_done")
        vec_in, cst_in, mem_in = sem("vec_in"), sem("cst_in"), sem("mem_in")
        x_in = [sem(f"x_in{i}") for i in range(4)]
        posted = sem("posted")
        acted, inner_made, acted_mix, m_out = (sem(n) for n in ("acted", "inner_made", "acted_mix", "ml_out"))
        dve_step, act_step, pe_step = sem("dve_step"), sem("act_step"), sem("pe_step")
        spilled, fetched = ([sem(f"{n}{i}") for i in range(2)] for n in ("spilled", "fetched"))
        rel_in, bias_psum, bias_sb, bias_out, toep_in = (sem(n) for n in ("rel_in", "bias_psum", "bias_sb", "bias_out", "toep_in"))
        v_ready, v_turned, v_stored = sem("v_ready"), sem("v_turned"), sem("v_stored")
        conv_in, gates_in, gates_turned, gates_out = (sem(n) for n in ("conv_in", "gates_in", "gates_turned", "gates_out"))
        gathered, hid_done, hid_bias, hid_act, cmp_proj, cmp_out = (sem(n) for n in ("gathered", "hid_done", "hid_bias", "hid_act", "cmp_proj", "cmp_out"))
        n_q, n_qk, n_add, n_exp, n_scaled, n_turned, n_pT, n_pv = (sem("nsa_" + n) for n in ("q", "qk", "add", "exp", "scaled", "turned", "pT", "pv"))
        m_row, m_col, m_colout, m_bc, m_floor, m_qk, m_diag, m_decay, m_weight, m_pv, m_h, m_sq, m_sum, m_root = (
            sem("ml_" + n) for n in ("row", "col", "colout", "bc", "floor", "qk", "diag", "decay", "weight", "pv", "h", "sq", "sum", "root"))
        m_soft, m_inv, m_factor, n_seen = sem("ml_soft"), sem("ml_inv"), sem("ml_factor"), sem("nsa_seen")
        x_qk, x_max, x_exp, x_scaled, x_turned, x_pT, x_pv = (sem("x_" + n) for n in ("qk", "max", "exp", "scaled", "turned", "pT", "pv"))
        c_glu, c_diag, c_pe, c_taps, c_product_made, c_product_used, c_conv, c_cent, c_norm = (
            sem("c_" + n) for n in ("glu", "diag", "pe", "taps", "product_made", "product_used", "conv", "cent", "norm"))
        s_v, s_vout, s_qk, s_clip, s_soft, s_log, s_sum, s_wt, s_pv, s_const, s_added = (
            sem("st_" + n) for n in ("v", "vout", "qk", "clip", "soft", "log", "sum", "wt", "pv", "const", "added"))
        last_out, out_done, w2_in = sem("last_out"), sem("out_done"), sem("w2_in")
        gb_in, bias_fill, pad_done, gather_part, gates_part, m_abs = (sem(n) for n in ("gb_in", "bias_fill", "pad_done", "gather_part", "gates_part", "ml_abs"))

        def cut(tile, k, w=S):
            return tile[:, bass.ds(k * w, w)]

        def col(name, c=0):
            return vec[:, bass.ds(c + VEC[name], 1)]

        def const(name, rows=P, lo=0, hi=None):
            size = dict(CONSTS)[name]
            return cst[0:rows, CST[name] + lo:CST[name] + (size if hi is None else hi)]

        ident = const("ident")
        ml_rows = [sq[0:4, 0:S], rB[0:4, :], sq[0:4, S:2 * S], acc[0:4, :], t0[0:4, :], t1[0:4, :]]
        def taps_done(pair, i, s):
            return 2 * (pair * (TAPS_DVE + 1) + i) + s + 1

        stage_blocks = {n: b for n, _, b in STAGES}
        V_IN = [8, 9, 10, 11, 12, 13]

        block = ctx.enter_context(nc.Block())

        @block.sync
        def _(sp):
            def load_x(i):
                sp.dma_start(cut(x, i, 2 * S), t["x"][:, 2 * i:2 * i + 2].rearrange("p c n -> p (c n)")).then_inc(x_in[i], 16)

            load_x(0)
            sp.dma_start(vec[:], t["vectors"]).then_inc(vec_in, 16)
            load_x(1)

            def load(slot, src, q):
                u = 4 * q + slot
                if not (isinstance(q, int) and u < RING):
                    sp.wait_ge(w_lo_made, u - 3)
                width = src.shape[-1]
                sp.dma_start(w_raw[:, slot * UNIT:slot * UNIT + width], src).then_inc(raw_in[slot], 16)

            def flat(w):
                return w.rearrange("u p k n -> u p (k n)")

            def stage(name, w):
                w = flat(w)
                q0 = U0[name] // RING
                for it in rounds(sp, w.shape[0] // RING):
                    for j in range(RING):
                        load(j, w[bass.ds(RING * it + j, 1)].rearrange("u p n -> (u p) n"), q0 + it)

            def stage_down(name, w):
                w = flat(w)
                q0 = U0[name] // RING
                for it in rounds(sp, KC // 4):
                    for j in range(12):
                        k0, kn = DN_KS[j % 3]
                        src = w[bass.ds(4 * it + j // 3, 1), :, k0 * P:(k0 + kn) * P].rearrange("u p n -> (u p) n")
                        load(j % RING, src, q0 + 3 * it + j // RING)

            w_in = flat(t["w_in"])
            for u in range(22):
                load(u % RING, w_in[u], u // RING)
                if u == 0:
                    load_x(2)
                    load_x(3)
                if u == 1:
                    sp.dma_start(cst[:], t["consts"]).then_inc(cst_in, 16)
            for j in range(2):
                load(2 + j, t["w_gates"].rearrange("p k n -> p (k n)")[:, j * 4 * P:(j + 1) * 4 * P], 5)
            stage("cmp", t["cmp_w1"])
            stage("out", t["w_out"])
            stage("xkv", t["w_xkv"])
            stage("xq", t["w_xq"])
            stage("xo", t["w_xo"])
            stage("gu0", t["w_gu0"])
            stage_down("dn0", t["w_dn0"])
            stage("gu1", t["w_gu1"])
            stage_down("dn1", t["w_dn1"])
            stage("pw1", t["w_pw1"])
            stage("pw2", t["w_pw2"])
            stage("gu2", t["w_gu2"])
            stage_down("dn2", t["w_dn2"])
            stage("kv", t["w_kv"])
            stage("gu3", t["w_gu3"])
            stage_down("dn3", t["w_dn3"])
            stage("q", t["w_q"])
            w_o = flat(t["w_o"])
            for u in range(RING):
                load(u, w_o[u], U0["o"] // RING)
            for par in range(2):
                sp.wait_ge(spilled[par], 16 * 12)
            for it in rounds(sp, KC // 2, peel=1):
                for j in range(2):
                    if not (isinstance(it, int) and it == 0):
                        sp.wait_ge(s_qk, 4 * it + 2 * j - 2)
                        sp.wait_ge(s_v, 2 * it + j - 1)
                    sp.dma_start(qkv[:, j * 3 * S:(j + 1) * 3 * S],
                                 qkv_dram[bass.ds(2 * it + j, 1)].rearrange("c p a n -> (c p) (a n)")).then_inc(fetched[j], 16)
            for u in range(RING, KC):
                load(u - RING, w_o[u], U0["o"] // RING + 1)
            stage("gu4", t["w_gu4"])
            stage_down("dn4", t["w_dn4"])

        @block.tensor
        def _(pe):
            def unit(q, j, dst, ks, hi, lo, start, stop, n=S, made=None, wait=op_lo):
                slot, q = j % RING, q + j // RING
                pe.wait_ge(w_lo_made, 4 * q + slot + 1)
                for i, k in enumerate(ks):
                    if made is not None:
                        pe.wait_ge(wait, made + k + 1)
                    at = slot * UNIT + i * P
                    parts = ((w_hi, hi), (w_lo, hi), (w_hi, lo))
                    for m, (w, o) in enumerate(parts):
                        last = nc.tensor.matmul(dst[:, 0:n], w[:, at:at + P], o[:, k * n:(k + 1) * n],
                                                start=start and i == 0 and m == 0,
                                                stop=stop and i == len(ks) - 1 and m == 2)
                last.then_inc(w_used, 1)

            def bank_free(b):
                if not (isinstance(b, int) and b < 4):
                    pe.wait_ge(evacuated, b - 3)

            def feature_sum(name, n=S):
                pe.wait_ge(summed, SUM0[name] + 9)
                nc.tensor.matmul(bank[7][:, 0:n], const("ones"), acc[:, 0:n], start=True, stop=True).then_inc(stat_done, 1)

            def dense(name, hi, lo, operand, norm=None, n=S):
                for it in rounds(pe, stage_blocks[name] // 4, peel=1):
                    for j in range(4):
                        bank_free(B0[name] + 4 * it + j)
                        first = isinstance(it, int) and it == 0 and j == 0
                        unit(U0[name] // 4 + it, j, bank[j], range(KC), hi, lo, True, True, n,
                             made=R0[operand] if first else None)
                        if first and norm:
                            feature_sum(norm, n)

            def down(name, f):
                for it in rounds(pe, KC // 4, peel=1):
                    for j in range(12):
                        b, r = divmod(j, 3)
                        k0, kn = DN_KS[r]
                        if r == 0:
                            bank_free(B0[name] + 4 * it + b)
                        first = isinstance(it, int) and it == 0 and b == 0
                        unit(U0[name] // 4 + 3 * it, j, bank[b], range(k0, k0 + kn), a_hi, a_lo, r == 0, r == 2,
                             made=FC * f if first else None, wait=f_lo)

            pe.wait_ge(rel_in, 16)
            pe.wait_ge(cst_in, 16)
            nc.tensor.matmul(bank[6][0:8, 0:S], onehot[0:32, S:S + 8], onehot[0:32, 0:S], start=True,
                             stop=True).then_inc(bias_psum, 1)

            idx = 0
            for b in range(22):
                bank_free(b)
                unit(b // 4, b % 4, bank[b % 4], range(KC), h_hi, h_lo, True, True, made=R0["mix"] if b == 0 else None)
                if b == 0:
                    feature_sum("mix")
                if b - 1 in V_IN:
                    pe.wait_ge(v_ready, idx + 1)
                    if idx >= 2:
                        pe.wait_ge(v_stored, idx - 1)
                    if idx == 1:
                        pe.wait_ge(bias_sb, 1)
                    src = (t0, t1)[idx % 2]
                    for k in range(TB):
                        last = nc.tensor.transpose(bank[5 + idx % 2][:, k * P:(k + 1) * P], src[:, k * P:(k + 1) * P], ident)
                    last.then_inc(v_turned, 1)
                    idx += 1
            bank_free(22)
            for j in range(2):
                slot = 2 + j
                pe.wait_ge(w_lo_made, 22 + j + 1)
                for i in range(4):
                    k = 4 * j + i
                    at = slot * UNIT + i * P
                    for m, (w, o) in enumerate(((w_hi, h_hi), (w_lo, h_hi), (w_hi, h_lo))):
                        last = nc.tensor.matmul(bank[2][:], w[:, at:at + P], cut(o, k), start=k == 0 and m == 0,
                                                stop=k == 7 and m == 2)
                last.then_inc(w_used, 1)
            pe.wait_ge(gates_in, 1)
            for k in range(TB):
                last = nc.tensor.transpose(bank[5][:, k * 24:(k + 1) * 24], gsb[0:24, k * P:(k + 1) * P], ident[0:24, 0:24])
            last.then_inc(gates_turned, 1)

            pe.wait_ge(evacuated, BEND["in"])
            for w in range(2):
                pe.wait_ge(op_lo, R0["cmp"] + w + 1)
                for uu in range(4):
                    pe.wait_ge(w_lo_made, U0["cmp"] + 4 * w + uu + 1)
                    for i in range(4):
                        g = (w * 16 + 4 * uu + i) * GW
                        for f in range(2):
                            at = uu * UNIT + (2 * i + f) * P
                            nc.tensor.matmul(bank[2 * w + f][:, 0:2 * GW], w_hi[:, at:at + P], g_hl[:, 2 * g:2 * g + 2 * GW],
                                             start=uu == 0 and i == 0, stop=False, skip_group_check=True)
                            last = nc.tensor.matmul(bank[2 * w + f][:, 0:GW], w_lo[:, at:at + P], g_hl[:, 2 * g:2 * g + GW],
                                                    start=False, stop=uu == 3 and i == 3, skip_group_check=True)
                    last.then_inc(w_used, 1)
            w2 = lambda w, f: cmp_w2[:, (2 * w + f) * DH:(2 * w + f + 1) * DH]
            hid = lambda w, f, h: cmp_h[:, (2 * w + f) * GW + h * NCMP:(2 * w + f) * GW + (h + 1) * NCMP]
            pe.wait_ge(hid_act, 2)
            pe.wait_ge(w2_in, 16)
            for h in range(2):
                for f in range(2):
                    nc.tensor.matmul(bank[4][h * DH:(h + 1) * DH, 0:NCMP], w2(0, f), hid(0, f, h), start=f == 0, stop=f == 1)
            pe.wait_ge(hid_act, 4)
            pe.wait_ge(gates_out, 1)
            for h in range(2):
                for f in range(2):
                    last = nc.tensor.matmul(bank[5][0:NCMP, h * DH:(h + 1) * DH], hid(1, f, h), w2(1, f), start=f == 0, stop=f == 1)
            last.then_inc(cmp_proj, 1)

            pe.wait_ge(cmp_out, 2)
            items, NI = NSA_ITEMS, len(NSA_ITEMS)
            for c in rounds(pe, 4):
                pe.wait_ge(n_q, c + 1)
                for s in range(NI + 3):
                    if s < NI:
                        half, qb, br = items[s]
                        rs = slice(half * DH, (half + 1) * DH)
                        n = (8 * qb + 7) if br == 0 else P * (qb + 1)
                        if s >= 2:
                            pe.wait_ge(n_add, NI * c + s - 1)
                        nc.tensor.matmul(bank[s % 2][:, 0:n], q_st[rs, qb * P:(qb + 1) * P],
                                         (kc, kS, kW)[br][rs, 0:n], start=True, stop=True).then_inc(n_qk, 1)
                    r = s - 2
                    if 0 <= r < NI:
                        half, qb, br = items[r]
                        pe.wait_ge(n_scaled, NI * c + r + 1)
                        if r >= 2:
                            pe.wait_ge(n_pT, NI * c + r - 1)
                        src, dst = p_sb[:, (r % 3) * S:(r % 3 + 1) * S], bank[2 + r % 2]
                        if br == 0:
                            n = 8 * qb + 7
                            last = nc.tensor.transpose(dst[0:n, 0:P], src[:, 0:n], ident)
                        else:
                            for k in range(qb + 1):
                                last = nc.tensor.transpose(dst[:, k * P:(k + 1) * P], src[:, k * P:(k + 1) * P], ident)
                        last.then_inc(n_turned, 1)
                    r = s - 3
                    if 0 <= r < NI:
                        half, qb, br = items[r]
                        pe.wait_ge(n_pT, NI * c + r + 1)
                        if r == 0:
                            pe.wait_ge(op_lo, R0["nsa"] + c)
                        dst = bank[4][half * DH:(half + 1) * DH, qb * P:(qb + 1) * P]
                        src = pT[:, (r % 2) * S:(r % 2 + 1) * S]
                        if br == 0:
                            n = 8 * qb + 7
                            last = nc.tensor.matmul(dst, vc[0:n, half * DH:(half + 1) * DH], src[0:n, 0:P], start=True, stop=False)
                        else:
                            for k in range(qb + 1):
                                at = k * 2 * P + (br - 1) * P + half * DH
                                last = nc.tensor.matmul(dst, v_nsa[:, at:at + DH], src[:, k * P:(k + 1) * P], start=False,
                                                        stop=br == 2 and k == qb)
                        last.then_inc(n_pv, 1)

            pe.wait_ge(m_row, 1)
            pe.wait_ge(acted_mix, 8)
            pe.wait_ge(op_lo, R0["nsa"] + 4)
            for k in range(TB):
                last = nc.tensor.transpose(bank[2][:, 4 * k:4 * k + 4], ml_rows[0][:, k * P:(k + 1) * P], ident[0:4, 0:4])
            last.then_inc(m_col, 1)
            pe.wait_ge(m_colout, 1)

            def ml_values(i):
                hd, kb = divmod(i, TB)
                pe.wait_ge(m_weight, i + 1)
                if kb == 0 and hd >= 2:
                    pe.wait_ge(m_h, hd - 1)
                n = S - kb * P
                src = weight[:, (i % 2) * S:(i % 2) * S + n]
                at = kb * 4 * P + hd * P
                nc.tensor.matmul(bank[4 + hd % 2][:, kb * P:S], v_ml[:, at:at + P], src, start=kb == 0, stop=kb == 3)
                nc.tensor.matmul(bank[6 + hd % 2][:, kb * P:S], const("ones"), src, start=kb == 0,
                                 stop=kb == 3).then_inc(m_pv, 1)

            for i in range(16):
                hd, kb = divmod(i, TB)
                if kb == 0:
                    if hd:
                        pe.wait_ge(m_decay, 4 * hd)
                        pe.wait_ge(m_floor, hd)
                    pick = const("pick", 4, hd * P, (hd + 1) * P)
                    nc.tensor.matmul(bank[0][:], pick, ml_rows[2], start=True, stop=True)
                    nc.tensor.matmul(bank[1][:], pick, ml_rows[3], start=True, stop=True).then_inc(m_bc, 1)
                if i >= 2:
                    pe.wait_ge(m_weight, i - 1)
                rs = slice((hd % 2) * DH, (hd % 2 + 1) * DH)
                k_at, q_at = (2 + hd // 2) * S + kb * P, (hd // 2) * S
                nc.tensor.matmul(bank[2 + i % 2][:, 0:S - kb * P], qk[rs, k_at:k_at + P], qk[rs, q_at + kb * P:q_at + S],
                                 start=True, stop=True).then_inc(m_qk, 1)
                if i >= 1:
                    ml_values(i - 1)
            ml_values(15)
            pe.wait_ge(m_h, 4)
            for hd in range(4):
                pe.wait_ge(m_sq, hd + 1)
                last = nc.tensor.matmul(bank[4][0:4, :], const("to_row", P, 4 * hd, 4 * hd + 4), cut(rows, hd), start=hd == 0, stop=hd == 3)
            last.then_inc(m_sum, 1)
            def out_parts(j, k):
                at = j * UNIT + k * P
                for m, (w, o) in enumerate(((w_hi, h_hi), (w_lo, h_hi), (w_hi, h_lo))):
                    last = nc.tensor.matmul(bank[j][:], w[:, at:at + P], cut(o, k), start=k == 0 and m == 0,
                                            stop=k == KC - 1 and m == 2)
                return last

            for j in range(4):
                bank_free(B0["out"] + j)
                pe.wait_ge(w_lo_made, U0["out"] + j + 1)
                for k in range(4):
                    out_parts(j, k)
                if j == 1:
                    pe.wait_ge(m_inv, 1)
                    for hd in range(4):
                        nc.tensor.matmul(bank[FACTOR_BANK[hd]][:], const("pick", 4, hd * P, (hd + 1) * P), rows[0:4, 4 * S:5 * S],
                                         start=True, stop=True).then_inc(m_factor, 1)
            for k in range(4, KC):
                pe.wait_ge(op_lo, R0["ml"] + k - 3)
                for j in range(4):
                    last = out_parts(j, k)
                    if k == KC - 1:
                        last.then_inc(w_used, 1)
            feature_sum("mem", MEM)
            for j in range(4):
                bank_free(B0["out"] + 4 + j)
                unit(U0["out"] // 4 + 1, j, bank[j], range(KC), h_hi, h_lo, True, True)
            for it in range(2):
                for j in range(4):
                    bank_free(B0["xkv"] + 4 * it + j)
                    unit(U0["xkv"] // 4 + it, j, bank[j], range(KC), m_hi, m_lo, True, True, MEM,
                         made=R0["mem"] if it == 0 and j == 0 else None)
                    if it == 0 and j == 0:
                        feature_sum("post_mix")
            for it in rounds(pe, 2):
                for j in range(5):
                    if j < 4:
                        bank_free(B0["xkv"] + 8 + 4 * it + j)
                        unit(U0["xkv"] // 4 + 2 + it, j, bank[j], range(KC), m_hi, m_lo, True, True, MEM)
                    if j:
                        i = 6 + 4 * it + j - 1
                        pe.wait_ge(v_ready, i + 1)
                        pe.wait_ge(v_stored, i - 1)
                        for k in range(2):
                            last = nc.tensor.transpose(bank[5 + (j - 1) % 2][:, k * P:(k + 1) * P],
                                                       (t0, t1)[(j - 1) % 2][:, k * P:(k + 1) * P], ident)
                        last.then_inc(v_turned, 1)
            dense("xq", h_hi, h_lo, "xq", "xq")
            pe.wait_ge(evacuated, BEND["xq"])
            pe.wait_ge(v_stored, 14)
            for s in range(16 + 2):
                if s < 16:
                    hd, qb = divmod(s, TB)
                    if s >= 2:
                        pe.wait_ge(x_exp, s - 1)
                    for k in range(2):
                        last = nc.tensor.matmul(bank[s % 2][:, 0:MEM], qx[:, (2 * hd + k) * S + qb * P:(2 * hd + k) * S + (qb + 1) * P],
                                                cut(kx, 2 * hd + k, MEM), start=k == 0, stop=k == 1)
                    last.then_inc(x_qk, 1)
                r = s - 2
                if r >= 0:
                    hd, qb = divmod(r, TB)
                    pe.wait_ge(x_scaled, r + 1)
                    if r >= 2:
                        pe.wait_ge(x_pT, r - 1)
                    for k in range(2):
                        last = nc.tensor.transpose(bank[2 + r % 2][:, k * P:(k + 1) * P],
                                                   px[:, (r % 3) * MEM + k * P:(r % 3) * MEM + (k + 1) * P], ident)
                    last.then_inc(x_turned, 1)
                    if qb == 3:
                        pe.wait_ge(x_pT, r + 1)
                        for dv in range(2):
                            c = 2 * hd + dv
                            if c >= 2:
                                pe.wait_ge(op_lo, R0["xo"] + c - 1)
                            for k in range(2):
                                last = nc.tensor.matmul(bank[4 + dv][:], vx[:, k * D + c * P:k * D + (c + 1) * P],
                                                        pxT[:, ((hd % 2) * 2 + k) * S:((hd % 2) * 2 + k + 1) * S],
                                                        start=k == 0, stop=k == 1)
                            last.then_inc(x_pv, 1)
            dense("xo", h_hi, h_lo, "xo")
            feature_sum("post_x")
            dense("gu0", h_hi, h_lo, "gu0", "gu0")
            down("dn0", 0)
            feature_sum("post_ffn")
            dense("gu1", h_hi, h_lo, "gu1", "gu1")
            down("dn1", 1)
            def taps(pair, j):
                i, c = j // 2, 2 * pair + j // 2
                if j % 2 == 0:
                    pe.wait_ge(c_glu, c + 1)
                    pe.wait_ge(c_diag, c + 1)
                    if not (isinstance(pair, int) and pair == 0):
                        pe.wait_ge(c_taps, taps_done(pair - 1, TAPS_DVE, i))
                for k in range(TAPS_PE * (j % 2) // 2, TAPS_PE * (j % 2 + 1) // 2):
                    last = nc.tensor.matmul(bank[4 + i][:], diag_w[:, (i * TAPS_PE + k) * P:(i * TAPS_PE + k + 1) * P],
                                            u_conv[:, bass.ds(c * (S + PAD) + k, S)], start=k == 0, stop=k == TAPS_PE - 1)
                if j % 2:
                    last.then_inc(c_pe, 1)

            for it in rounds(pe, KC // 2, peel=2):
                first = isinstance(it, int) and it == 0
                for j in range(4):
                    bank_free(B0["pw1"] + 4 * it + j)
                    unit(U0["pw1"] // 4 + it, j, bank[j], range(KC), h_hi, h_lo, True, True,
                         made=R0["pw1"] if first and j == 0 else None)
                    if first and j == 0:
                        feature_sum("pw1")
                    if not first:
                        taps(it - 1, j)
            for j in range(4):
                taps(KC // 2 - 1, j)
            pe.wait_ge(root_done, NORM["pw1"] + 1)
            for c in range(KC):
                pe.wait_ge(c_conv, c + 1)
                last = nc.tensor.matmul(bank[7][:], const("ones"), cut(cv, c), start=c == 0, stop=c == KC - 1)
            last.then_inc(stat_done, 1)
            feature_sum("ln_var")
            dense("pw2", o_hi, o_lo, "pw2")
            dense("gu2", h_hi, h_lo, "gu2", "gu2")
            down("dn2", 2)
            dense("kv", h_hi, h_lo, "kv", "kv")
            dense("gu3", h_hi, h_lo, "gu3")
            down("dn3", 3)
            dense("q", h_hi, h_lo, "q", "q")

            def stick_scores(it, jj):
                g, p, j = 4 * it + jj, 2 * it + jj // 2, jj // 2
                rs = slice(jj % 2 * DH, (jj % 2 + 1) * DH)
                qT_, kT, vT = (qkv[:, (3 * j + m) * S:(3 * j + m + 1) * S] for m in range(3))
                if jj % 2 == 0:
                    pe.wait_ge(fetched[j], 16 * (it + 1))
                if not (isinstance(it, int) and it == 0 and jj < 2):
                    pe.wait_ge(s_wt, g - 1)
                z = banks[jj % 2]
                for kb, (at, n) in STICKS.items():
                    nc.tensor.matmul(z[:, at:at + n], kT[rs, kb * P:(kb + 1) * P], qT_[rs, kb * P:S],
                                     start=kb != 3, stop=False, skip_group_check=True)
                    last = nc.tensor.matmul(z[:, at:at + P], mask_b[:], ident_b[:], start=False, stop=False,
                                            skip_group_check=True)
                last.then_inc(s_qk, 1)
                if jj % 2 == 0:
                    if not (isinstance(it, int) and it == 0 and jj == 0):
                        pe.wait_ge(s_vout, p)
                    for k in range(TB):
                        last = nc.tensor.transpose(bank[7][:, k * P:(k + 1) * P], vT[:, k * P:(k + 1) * P], ident)
                    last.then_inc(s_v, 1)

            def stick_sums(g, jj):
                pe.wait_ge(s_soft, g + 1)
                z, l0, a0 = banks[jj % 2], jj % 2 * STICK, jj % 2 * 3 * P
                for kb, (at, n) in STICKS.items():
                    nc.tensor.matmul(z[:, at:at + n], const("minus_from_here"), s_l[:, l0 + at:l0 + at + n],
                                     start=False, stop=kb == 3, skip_group_check=True)
                for kb in range(3):
                    at, k_at = STICKS[kb][0] + P, l0 + STICKS[kb + 1][0]
                    nc.tensor.matmul(z[:, at:at + P], const("minus_ones"), s_l[:, k_at:k_at + P],
                                     start=False, stop=kb == 2, skip_group_check=True)
                pe.wait_ge(s_added, 3 * g + 3)
                for kb, lo, n in ((1, 0, P), (0, P, 2 * P)):
                    at = STICKS[kb][0] + 2 * P
                    last = nc.tensor.matmul(z[:, at:at + n], const("minus_ones"), s_later[:, a0 + lo:a0 + lo + n],
                                            start=False, stop=True, skip_group_check=True)
                last.then_inc(s_sum, 1)

            def stick_values(it, jj):
                g, p = 4 * it + jj, 2 * it + jj // 2
                half, vb = jj % 2, jj // 2 % 2
                pe.wait_ge(s_wt, g + 1)
                if half == 0:
                    pe.wait_ge(s_vout, p + 1)
                    pe.wait_ge(op_lo, R0["o"] + p)
                src, dst = s_w[:, half * STICK:(half + 1) * STICK], bank[3][half * DH:(half + 1) * DH, :]
                for kb in reversed(range(TB)):
                    at, n = STICKS[kb]
                    v_at = vb * S + kb * P + half * DH
                    last = nc.tensor.matmul(dst[:, kb * P:(kb + 1) * P], v_st[:, v_at:v_at + DH], src[:, at:at + P],
                                            start=kb == 3, stop=kb == 0, skip_group_check=True)
                    if kb < 3:
                        last = nc.tensor.matmul(dst[:, (kb + 1) * P:S], v_st[:, v_at:v_at + DH], src[:, at + P:at + n],
                                                start=False, stop=kb == 0, skip_group_check=True)
                last.then_inc(s_pv, 1)

            pe.wait_ge(evacuated, BEND["q"])
            pe.wait_ge(s_const, 2)
            for it in rounds(pe, KC // 2, peel=1):
                first = isinstance(it, int) and it == 0
                for jj in range(4):
                    stick_scores(it, jj)
                    if not (first and jj == 0):
                        stick_sums(4 * it + jj - 1, jj - 1)
                    if not (first and jj < 2):
                        stick_values(it, jj - 2)
            stick_sums(2 * KC - 1, 3)
            stick_values(KC // 2 - 1, 2)
            stick_values(KC // 2 - 1, 3)
            dense("o", o_hi, o_lo, "o")
            dense("gu4", h_hi, h_lo, "gu4", "gu4")
            down("dn4", 4)
            feature_sum("final")

        @block.scalar
        def _(act):
            steps = Steps(act, act_step)

            def split(name, it, per, j):
                q, slot = U0[name] // RING + it * (per // RING) + j // RING, j % RING
                if isinstance(q, int) and 4 * q + slot >= UNITS:
                    return
                act.wait_ge(raw_in[slot], 16 * (q + 1))
                if not (isinstance(q, int) and q == 0):
                    act.wait_ge(w_used, 4 * q + slot - 3)
                nc.scalar.activation(cut(w_hi, slot, UNIT), cut(w_raw, slot, UNIT), ACT.Copy).then_inc(w_hi_made, 1)

            def chunk(norm, c, k, gain, src=x, hi=h_hi, n=S):
                if not (isinstance(c, int) and c == 0 and NORM[norm] == 0):
                    act.wait_ge(summed, SUM0[norm] + c)
                nc.scalar.activation(sq[:, (k % 2) * S:(k % 2) * S + n], cut(src, c, n), ACT.Square).then_inc(squared, 1)
                if gain is not None:
                    nc.scalar.activation(cut(hi, c, n), cut(src, c, n), ACT.Copy, scale=col(gain, c)).then_inc(op_hi, 1)

            def root(name, dst=rB, n=S, eps="norm_eps"):
                act.wait_ge(stat_done, NORM[name] + 1)
                nc.scalar.activation(dst[:, 0:n], bank[7][:, 0:n], ACT.Sqrt, scale=1.0 / D, bias=const(eps)).then_inc(root_done, 1)

            def stage(name, norm=None, after=None, per=4, peel=0):
                n_it = (UEND[name] - U0[name]) // per
                for it in rounds(act, n_it, peel=max(peel, 1 if norm else 0)):
                    for j in range(per):
                        split(name, it, per, j + 2)
                        if isinstance(it, int) and it == 0 and j == 0 and norm:
                            root(norm)
                        if after:
                            after(it, j)

            def gate_up(name, f, norm):
                def inner(it, j):
                    if j % 2:
                        c = 2 * it + j // 2
                        act.wait_ge(evacuated, B0[name] + 4 * it + j)
                        nc.scalar.activation(t0[:], t0[:], ACT.Silu).then_inc(acted, 1)
                        act.wait_ge(inner_made, FC * f + c + 1)
                        nc.scalar.activation(cut(a_hi, c), t1[:], ACT.Copy).then_inc(f_hi, 1)
                stage(name, norm, inner)

            def down(name, norm, gain, src=x):
                def result(it, j):
                    if j % 3 == 2:
                        c = 4 * it + j // 3
                        act.wait_ge(evacuated, B0[name] + c + 1)
                        chunk(norm, c, j // 3, gain, src)
                stage(name, None, result, per=12, peel=2 if name == "dn4" else 0)

            def post(norm, base, gain):
                for c in range(KC):
                    act.wait_ge(posted, base + c + 1)
                    chunk(norm, c, c, gain)

            act.wait_ge(vec_in, 16)
            for c in range(KC):
                act.wait_ge(x_in[c // 2], 16)
                chunk("mix", c, c, "mix_norm_pre")
                if c % 4 == 3:
                    split("in", 0, 4, c // 4)
            act.wait_ge(cst_in, 16)

            for u in range(24):
                split("in", 0, 4, u + 2)
                if u == 0:
                    root("mix")
                b = u - 1
                if b in (4, 5):
                    w = b - 4
                    act.wait_ge(gathered, w + 1)
                    nc.scalar.activation(g_parts[:, w, :, 0], g_raw[:].rearrange("p (j n) -> p j n", n=GW), ACT.Copy).then_inc(op_hi, 1)
                if 14 <= b < 18:
                    act.wait_ge(conv_in, b - 13)
                    nc.scalar.activation(cut(qk, b - 14), cut(qk, b - 14), ACT.Silu, bias=col("conv_b", b - 14)).then_inc(acted_mix, 1)
                if 18 <= b < 22:
                    act.wait_ge(evacuated, b + 1)
                    nc.scalar.activation(cut(mo, b - 18), cut(mo, b - 18), ACT.Sigmoid).then_inc(acted_mix, 1)
            act.wait_ge(evacuated, BEND["in"])
            nc.scalar.activation(gsb[0:24, :], gsb[0:24, :], ACT.Sigmoid).then_inc(gates_in, 1)

            def hidden(w):
                for f in range(2):
                    act.wait_ge(hid_bias, 2 * w + f + 1)
                    at = (2 * w + f) * GW
                    nc.scalar.activation(cmp_h[:, at:at + 2 * NCMP], cmp_h[:, at:at + 2 * NCMP], ACT.Silu,
                                         bias=cmp_h[:, at + 2 * NCMP:at + 2 * NCMP + 1]).then_inc(hid_act, 1)

            for u in range(8):
                split("cmp", 0, 4, u + 2)
                if u == 3:
                    act.wait_ge(m_abs, 2)
                    steps.done(nc.scalar.activation(ml_rows[4], ml_rows[4], ACT.Exp, scale=-1.0))
                    nc.scalar.activation(ml_rows[4], ml_rows[4], ACT.Ln, bias=const("one", 4)).then_inc(m_soft, 1)
                if u == 5:
                    hidden(0)
            hidden(1)
            for u in (8, 9):
                split("cmp", 0, 4, u + 2)

            items, NI = NSA_ITEMS, len(NSA_ITEMS)
            for c in rounds(act, 4):
                for s in range(NI + 2):
                    if s < NI:
                        half, qb, br = items[s]
                        n = (8 * qb + 7) if br == 0 else P * (qb + 1)
                        act.wait_ge(n_add, NI * c + s + 1)
                        if s >= 3:
                            act.wait_ge(n_turned, NI * c + s - 2)
                        nc.scalar.activation(p_sb[:, (s % 3) * S:(s % 3) * S + n], s_sb[:, (s % 2) * S:(s % 2) * S + n], ACT.Exp,
                                             scale=-1.0, bias=small[:, 8 + s % 2:9 + s % 2],
                                             accum_out=small[:, 12 + s % 2:13 + s % 2]).then_inc(n_exp, 1)
                    r = s - 2
                    if r >= 0:
                        half, qb, br = items[r]
                        act.wait_ge(n_turned, NI * c + r + 1)
                        if r >= 2:
                            act.wait_ge(n_pv, NI * c + r - 1)
                        rows_n, n = (8 * qb + 7, P) if br == 0 else (P, P * (qb + 1))
                        nc.scalar.activation(pT[0:rows_n, (r % 2) * S:(r % 2) * S + n], bank[2 + r % 2][0:rows_n, 0:n],
                                             ACT.Copy).then_inc(n_pT, 1)
                act.wait_ge(n_pv, NI * c + NI)
                nc.scalar.activation(cut(h_hi, c), bank[4][:], ACT.Copy).then_inc(op_hi, 1)

            for i in range(16):
                hd, kb = divmod(i, TB)
                dst = decay[:, (i % 2) * S:(i % 2 + 1) * S]
                if i >= 2:
                    act.wait_ge(m_weight, i - 1)
                act.wait_ge(m_diag, i + 1)
                last = nc.scalar.activation(dst[:, 0:P], diag[:, (i % 2) * P:(i % 2 + 1) * P], ACT.Exp)
                if kb < 3:
                    last = nc.scalar.activation(dst[:, P:S - kb * P], bank[0][:, (kb + 1) * P:S], ACT.Exp,
                                                bias=a_col[:, 4 * kb + hd:4 * kb + hd + 1])
                last.then_inc(m_decay, 1)
                if kb == 3:
                    if hd:
                        act.wait_ge(m_h, hd)
                    nc.scalar.activation(floor[:], bank[1][:], ACT.Exp).then_inc(m_floor, 1)
            for hd in range(4):
                act.wait_ge(m_h, hd + 1)
                nc.scalar.activation(cut(rows, hd), cut(h_ml, hd), ACT.Square).then_inc(m_sq, 1)
            act.wait_ge(m_sum, 1)
            nc.scalar.activation(rows[0:4, 4 * S:5 * S], bank[4][0:4, :], ACT.Sqrt, scale=1.0 / P,
                                 bias=const("norm_eps", 4)).then_inc(m_root, 1)
            for hd in range(4):
                act.wait_ge(m_out, hd + 1)
                nc.scalar.activation(cut(h_hi, 4 + hd), cut(h_ml, hd), ACT.Copy).then_inc(op_hi, 1)
            act.wait_ge(mem_in, 16)
            for c in range(KC):
                chunk("mem", c, c, "mem_norm", mem, m_hi, MEM)

            for u in range(8):
                if u >= 2:
                    split("out", 0, 4, u + 2)
                if u == 0:
                    root("mem", rM, MEM)
                act.wait_ge(evacuated, B0["out"] + u + 1)
                chunk("post_mix", u, u, None, yb_x)

            for u in range(8):
                split("xkv", 0, 4, u + 2)
                if u == 0:
                    root("post_mix")
                else:
                    act.wait_ge(posted, u)
                    chunk("xq", u - 1, u - 1, "xattn_norm_pre")
            act.wait_ge(posted, KC)
            chunk("xq", KC - 1, KC - 1, "xattn_norm_pre")
            for it in rounds(act, 2):
                for j in range(4):
                    split("xkv", it + 2, 4, j + 2)
            stage("xq", "xq")
            for s in range(16 + 2):
                if s < 16:
                    if s >= 3:
                        act.wait_ge(x_turned, s - 2)
                    act.wait_ge(x_max, s + 1)
                    nc.scalar.activation(cut(px, s % 3, MEM), bank[s % 2][:, 0:MEM], ACT.Exp, bias=small[:, 8 + s % 2:9 + s % 2],
                                         accum_out=small[:, 12 + s % 2:13 + s % 2]).then_inc(x_exp, 1)
                r = s - 2
                if r >= 0:
                    hd, qb = divmod(r, TB)
                    act.wait_ge(x_turned, r + 1)
                    if qb == 0 and hd >= 2:
                        act.wait_ge(x_pv, 2 * hd - 2)
                    for k in range(2):
                        at = ((hd % 2) * 2 + k) * S + qb * P
                        last = nc.scalar.activation(pxT[:, at:at + P], bank[2 + r % 2][:, k * P:(k + 1) * P], ACT.Copy)
                    last.then_inc(x_pT, 1)
                    if qb == 3:
                        for dv in range(2):
                            act.wait_ge(x_pv, 2 * hd + dv + 1)
                            nc.scalar.activation(cut(h_hi, 2 * hd + dv), bank[4 + dv][:], ACT.Copy).then_inc(op_hi, 1)

            def result_yb(it, j):
                act.wait_ge(evacuated, B0["xo"] + 4 * it + j + 1)
                chunk("post_x", 4 * it + j, j, None, yb_x)
            stage("xo", None, result_yb)
            root("post_x")
            post("gu0", 8, "ffn_norm_pre")
            gate_up("gu0", 0, "gu0")
            down("dn0", "post_ffn", None, yb_h)
            root("post_ffn")
            post("gu1", 16, "ffn1_0")
            gate_up("gu1", 1, "gu1")
            down("dn1", "pw1", "mix_0")

            def products(pair, n0, n1):
                for n in range(n0, n1):
                    s, i = divmod(n, TAPS_POOL)
                    c, k = 2 * pair + s, TAPS_PE + i
                    at = 2 * TAPS_POOL * pair + n
                    if i == 0:
                        act.wait_ge(c_glu, c + 1)
                    if not (isinstance(pair, int) and pair == 0 and n < 2):
                        act.wait_ge(c_product_used, at - 1)
                    nc.scalar.activation(cut(c_product, n % 2), u_conv[:, bass.ds(c * (S + PAD) + k, S)], ACT.Identity,
                                         scale=col("w_dw", c * TAPS + k),
                                         bias=col("b_dw", c) if i == 0 else const("zero")).then_inc(c_product_made, 1)

            def diagonals(c, slot):
                if not (isinstance(c, int) and c < 2):
                    act.wait_ge(c_pe, c - 1)
                for k in range(TAPS_PE):
                    at = (slot * TAPS_PE + k) * P
                    last = nc.scalar.activation(diag_w[:, at:at + P], ident, ACT.Copy, scale=col("w_dw", c * TAPS + k))
                last.then_inc(c_diag, 1)

            def glu(it, j):
                first = isinstance(it, int) and it == 0
                if first and j == 0:
                    act.wait_ge(w_used, UEND["dn1"])
                if j == 0 and not first:
                    diagonals(2 * it - 1, 1)
                if j == 2:
                    diagonals(2 * it, 0)
                if not first:
                    products(it - 1, 2 * TAPS_POOL * j // 4, 2 * TAPS_POOL * (j + 1) // 4)
                if j % 2:
                    act.wait_ge(evacuated, B0["pw1"] + 4 * it + j + 1)
                    nc.scalar.activation(t0[:], t0[:], ACT.Sigmoid, bias=col("b_pw1", 8 + 2 * it + j // 2)).then_inc(acted, 1)
            stage("pw1", "pw1", glu, peel=2)
            diagonals(KC - 1, 1)
            products(KC // 2 - 1, 0, 2 * TAPS_POOL)
            act.wait_ge(stat_done, NORM["ln_mean"] + 1)
            nc.scalar.activation(rB[:], bank[7][:], ACT.Copy, scale=1.0 / D).then_inc(root_done, 1)
            for c in range(KC):
                act.wait_ge(c_cent, c + 1)
                chunk("ln_var", c, c, None, cv)
            root("ln_var", eps="ln_eps")
            for c in range(KC):
                act.wait_ge(c_norm, c + 1)
                steps.done(nc.scalar.activation(cut(cv, c), cut(cv, c), ACT.Silu, scale=col("ln_g", c), bias=col("ln_b", c)))
                nc.scalar.activation(cut(o_hi, c), cut(cv, c), ACT.Copy).then_inc(op_hi, 1)

            def result(name, norm, gain):
                def after(it, j):
                    act.wait_ge(evacuated, B0[name] + 4 * it + j + 1)
                    chunk(norm, 4 * it + j, j, gain)
                stage(name, None, after)

            result("pw2", "gu2", "ffn2_0")
            gate_up("gu2", 2, "gu2")
            down("dn2", "kv", "kv_norm")

            for m, m0 in ((1, 0), (2, 8)):
                for it in rounds(act, 2, peel=1 if m == 1 else 0):
                    for j in range(4):
                        split("kv", it + m0 // 4, 4, j + 2)
                        if m == 1 and isinstance(it, int) and it == 0 and j == 0:
                            root("kv")
                        act.wait_ge(evacuated, B0["kv"] + m0 + 4 * it + j + 1)
                        act.dma_start(qkv_dram[bass.ds(4 * it + j, 1), :, m, :].rearrange("c p n -> (c p) n"),
                                      (t0, t1)[j % 2][:]).then_inc(spilled[j % 2], 16)
            act.wait_ge(w_used, UEND["kv"])
            for c in range(KC):
                nc.scalar.activation(cut(h_hi, c), cut(x, c), ACT.Copy, scale=col("ffn1_1", c)).then_inc(op_hi, 1)
            gate_up("gu3", 3, None)
            down("dn3", "q", "mix_1")
            for it in rounds(act, 2, peel=1):
                for j in range(4):
                    split("q", it, 4, j + 2)
                    if isinstance(it, int) and it == 0 and j == 0:
                        root("q")
                    act.wait_ge(evacuated, B0["q"] + 4 * it + j + 1)
                    act.dma_start(qkv_dram[bass.ds(4 * it + j, 1), :, 0, :].rearrange("c p n -> (c p) n"),
                                  (t0, t1)[j % 2][:]).then_inc(spilled[j % 2], 16)

            def stick_weights(g, jj, first=False):
                act.wait_ge(s_sum, g + 1)
                if not first:
                    act.wait_ge(s_pv, g - 1)
                nc.scalar.activation(s_w[:, jj % 2 * STICK:(jj % 2 + 1) * STICK], banks[jj % 2][:, 0:STICK],
                                     ACT.Exp).then_inc(s_wt, 1)

            def stick_out(p):
                act.wait_ge(s_pv, 2 * p + 2)
                nc.scalar.activation(cut(o_hi, p), bank[3][:], ACT.Copy).then_inc(op_hi, 1)

            for it in steps.loop(KC // 2, 4, peel=1):
                first = isinstance(it, int) and it == 0
                for jj in range(4):
                    g = 4 * it + jj
                    e = s_l[:, jj % 2 * STICK:(jj % 2 + 1) * STICK]
                    act.wait_ge(s_clip, g + 1)
                    steps.done(nc.scalar.activation(e, e, ACT.Exp))
                    if not (first and jj == 0):
                        stick_weights(g - 1, jj - 1, first and jj < 3)
                    nc.scalar.activation(e, e, ACT.Ln, bias=const("one")).then_inc(s_log, 1)
                    if jj % 2 == 0:
                        act.wait_ge(s_v, 2 * it + jj // 2 + 1)
                        if not first:
                            act.wait_ge(s_pv, g - 2)
                        nc.scalar.activation(cut(v_st, jj // 2), bank[7][:], ACT.Copy).then_inc(s_vout, 1)
                    elif not (first and jj == 1):
                        stick_out(2 * it + jj // 2 - 1)
            stick_weights(2 * KC - 1, 3)
            stick_out(KC - 1)
            result("o", "gu4", "ffn2_1")
            gate_up("gu4", 4, "gu4")
            down("dn4", "final", None)
            root("final")
            for c in range(KC):
                act.wait_ge(last_out, c + 1)
                act.dma_start(out[:, c * S:(c + 1) * S], cut(x, c)).then_inc(out_done, 16)
            act.wait_ge(out_done, 16 * KC)

        @block.vector
        def _(dve):
            steps = Steps(dve, dve_step)
            V = nc.vector

            def split(name, it, per, j):
                q, slot = U0[name] // RING + it * (per // RING) + j // RING, j % RING
                if isinstance(q, int) and 4 * q + slot >= UNITS:
                    return
                dve.wait_ge(w_hi_made, 4 * q + slot + 1)
                V.tensor_tensor(cut(w_lo, slot, UNIT), cut(w_raw, slot, UNIT), cut(w_hi, slot, UNIT).bitcast(f32), sub).then_inc(w_lo_made, 1)

            def lo_part(operand, c, gain, src=x, hi=h_hi, lo=h_lo, n=S):
                dve.wait_ge(op_hi, R0[operand] + c + 1)
                hi_c = cut(hi, c, n).bitcast(f32)
                if gain is None:
                    V.tensor_tensor(cut(lo, c, n), cut(src, c, n), hi_c, sub).then_inc(op_lo, 1)
                else:
                    V.scalar_tensor_tensor(cut(lo, c, n), cut(src, c, n), col(gain, c), hi_c, mult, sub).then_inc(op_lo, 1)

            def factor(name, dst=rB, n=S):
                dve.wait_ge(root_done, NORM[name] + 1)
                return V.reciprocal(dst[:, 0:n], dst[:, 0:n])

            def scaled(dst, src, r=None, by=None):
                r = rB[:] if r is None else r
                if by is None:
                    return V.tensor_tensor(dst, src, r, mult)
                return V.scalar_tensor_tensor(dst, src, by, r, mult, mult)

            def stage(name, norm, result, per=4, peel=0, count=0):
                n_it = (UEND[name] - U0[name]) // per
                peel = max(peel, 1 if norm else 0)
                if norm:
                    split(name, 0, per, 2)
                    steps.done(factor(norm))
                for it in steps.loop(n_it, count, peel):
                    for j in range(per):
                        if not (norm and isinstance(it, int) and it == 0 and j == 0):
                            split(name, it, per, j + 2)
                        dve.wait_ge(w_used, U0[name] + per * it + j + 1)
                        result(it, j)

            def gate_up(name, f, norm):
                def inner(it, j):
                    c = 2 * it + j // 2
                    b = B0[name] + 4 * it + j
                    if j % 2 and not (isinstance(c, int) and FC * f + c == 0):
                        dve.wait_ge(f_lo, FC * f + c)
                    scaled((t0, t1)[j % 2][:], bank[j][:]).then_inc(evacuated, 1)
                    if j % 2:
                        dve.wait_ge(acted, ACTED0[name] + c + 1)
                        dve.wait_ge(evacuated, b + 1)
                        V.tensor_tensor(t1[:], t0[:], t1[:], mult).then_inc(inner_made, 1)
                        dve.wait_ge(f_hi, FC * f + c + 1)
                        V.tensor_tensor(cut(a_lo, c), t1[:], cut(a_hi, c).bitcast(f32), sub).then_inc(f_lo, 1)
                stage(name, norm, inner)

            def down(name, operand, gain, by=0.5):
                def result(it, j):
                    if j % 3 == 2:
                        c = 4 * it + j // 3
                        V.scalar_tensor_tensor(cut(x, c), bank[j // 3][:], by, cut(x, c), mult, add).then_inc(evacuated, 1)
                        if gain is None:
                            return
                        lo_part(operand, c, gain)
                stage(name, None, result, per=12, peel=2 if name == "dn4" else 0)

            def post_chunk(c, yb, gain):
                dst = (t0, t1)[c % 2]
                steps.done(V.scalar_tensor_tensor(dst[:], cut(yb, c), col(gain, c), rB[:], mult, mult))
                V.tensor_tensor(cut(x, c), cut(x, c), dst[:], add).then_inc(posted, 1)

            def post(norm, yb, gain, operand, gain_next):
                steps.done(factor(norm))
                for c in range(KC + 1):
                    if c < KC:
                        post_chunk(c, yb, gain)
                    if c:
                        lo_part(operand, c - 1, gain_next)

            def backwards(half):
                return toep_st[:, half * S:(half + 1) * S][:, ::-1]

            def turn_in(i, par, dst, n):
                dve.wait_ge(v_turned, i + 1)
                V.tensor_copy(dst, bank[5 + par][:, 0:n].rearrange("p (b f) -> p b f", f=P)).then_inc(v_stored, 1)

            V.memset(r_bias[:, 0:P], NEG).then_inc(bias_fill, 1)
            dve.wait_ge(vec_in, 16)
            for c in range(KC):
                dve.wait_ge(x_in[c // 2], 16)
                lo_part("mix", c, "mix_norm_pre")
                if c % 4 == 3:
                    split("in", 0, 4, c // 4)
            dve.wait_ge(cst_in, 16)
            dve.wait_ge(bias_psum, 1)
            V.tensor_copy(r_bias[0:8, P:HBM_BIAS], bank[6][0:8, :]).then_inc(bias_sb, 1)
            V.memset(u_pad[:], 0.0).then_inc(pad_done, 1)
            V.memset(g_raw[:], 0.0).then_inc(pad_done, 1)

            split("in", 0, 4, 2)
            steps.done(factor("mix"))
            dve.wait_ge(pad_done, 2)
            idx = 0
            for b in range(22):
                if b:
                    split("in", 0, 4, b + 2)
                dve.wait_ge(w_used, b + 1)
                src = bank[b % 4][:]
                if b < 4:
                    scaled(cut(qT, b), src, by=DH ** -0.5).then_inc(evacuated, 1)
                elif b < 6:
                    w = b - 4
                    scaled(t0[:], src).then_inc(evacuated, 1)
                    dve.wait_ge(evacuated, b + 1)
                    if w:
                        dve.wait_ge(op_lo, R0["cmp"] + 1)
                    g = g_raw[:].rearrange("p (j n) -> p j n", n=GW)
                    for par in range(2):
                        for head in range(2):
                            s4 = t0[head * DH:(head + 1) * DH, :].rearrange("p (ch m e) -> p e m ch", e=2, m=8)[:, par]
                            for late in range(2):
                                V.tensor_copy(g[par * DH:(par + 1) * DH, 8 * late:8 * late + 8, head * NCMP:(head + 1) * NCMP],
                                              s4[:, :, late:late + NCMP]).then_inc(gather_part, 1)
                    V.tensor_copy(g[:, :, 2 * NCMP:2 * NCMP + 1],
                                  vec[:, VEC["pos_k"] + 16 * w:VEC["pos_k"] + 16 * w + 16].unsqueeze(2)).then_inc(gather_part, 1)
                    dve.wait_ge(gather_part, 9 * (w + 1))
                    dve.sem_inc(gathered, 1)
                    dve.wait_ge(op_hi, R0["cmp"] + w + 1)
                    V.tensor_tensor(g_parts[:, w, :, 1], g, g_parts[:, w, :, 0].bitcast(f32), sub).then_inc(op_lo, 1)
                elif b < 8:
                    scaled((kS, kW)[b - 6][:], src).then_inc(evacuated, 1)
                elif b < 14:
                    if idx >= 2:
                        dve.wait_ge(v_turned, idx - 1)
                    scaled((t0, t1)[idx % 2][:], src).then_inc(evacuated, 1)
                    dve.wait_ge(evacuated, b + 1)
                    dve.sem_inc(v_ready, 1)
                elif b < 18:
                    c = b - 14
                    u = u_pad[:, c * (S + 3):(c + 1) * (S + 3)]
                    scaled(u[:, 3:], src).then_inc(evacuated, 1)
                    dve.wait_ge(evacuated, b + 1)
                    for k in range(4):
                        w = col("conv_w", 4 * c + k)
                        if k == 0:
                            last = V.tensor_scalar(cut(qk, c), u[:, 0:S], w, None, mult)
                        else:
                            last = V.scalar_tensor_tensor(cut(qk, c), u[:, k:k + S], w, cut(qk, c), mult, add)
                        if k < 3:
                            steps.done(last)
                    last.then_inc(conv_in, 1)
                else:
                    if b == 18:
                        dve.wait_ge(bias_out, 16)
                    scaled(cut(mo, b - 18), src).then_inc(evacuated, 1)
                if b - 2 in V_IN:
                    i = b - 2 - V_IN[0]
                    width, at = (2 * P, i * P) if i < 2 else (4 * P, (i - 2) * P)
                    tile = v_nsa if i < 2 else v_ml
                    turn_in(i, i % 2, tile[:].rearrange("p (b f) -> p b f", f=width)[:, :, at:at + P], S)
                if b in V_IN:
                    idx += 1
            split("in", 0, 4, 24)
            dve.wait_ge(w_used, 24)
            split("in", 0, 4, 25)
            for k in range(2):
                scaled(gsb[:, k * 256:(k + 1) * 256], bank[2][:, k * 256:(k + 1) * 256], rB[:, k * 256:(k + 1) * 256]).then_inc(evacuated, 1)
            dve.wait_ge(gates_turned, 1)
            V.tensor_copy(gate[:], bank[5][:, 0:TB * 24]).then_inc(gates_part, 1)
            dve.wait_ge(gates_part, 1)
            g0 = gate[:, 0:24].rearrange("p (h r) -> p h r", r=3)[:, :, 0]
            V.tensor_scalar(g0, g0, const("has_block"), None, mult).then_inc(gates_out, 1)

            def hidden_bias(w):
                for f in range(2):
                    dst = cut(cmp_h, 2 * w + f, GW)
                    steps.done(V.tensor_copy(dst, bank[2 * w + f][:, GW:2 * GW]))
                    V.tensor_tensor(dst, bank[2 * w + f][:, 0:GW], dst, add).then_inc(hid_bias, 1)

            row = lambda k: ml_rows[k]

            def gate_rows_1():
                dve.wait_ge(gb_in, 16)
                bi, bf = gbias[0:4, 0:1], gbias[0:4, 1:2]
                steps.done(V.tensor_copy(row(0), gsb[MI:MI + 4, :]))
                steps.done(V.tensor_copy(row(1), gsb[MF:MF + 4, :]))
                steps.done(V.tensor_scalar(row(0), row(0), bi, None, add))
                steps.done(V.tensor_scalar(row(1), row(1), bf, None, add))
                V.scalar_tensor_tensor(row(4), row(1), -1.0, row(1), mult, amax).then_inc(m_abs, 1)
                V.memset(row(5), 0.0).then_inc(m_abs, 1)

            def gate_rows_2():
                dve.wait_ge(m_soft, 1)
                dve.wait_ge(m_abs, 2)
                steps.done(V.scalar_tensor_tensor(row(1), row(1), 0.0, row(4), amin, sub))
                steps.done(V.tensor_tensor_scan(row(2), row(1), row(5), 0.0, add, amin))
                steps.done(V.tensor_copy(row(1), row(2)))
                steps.done(V.tensor_tensor(row(0), row(0), row(1), sub))
                steps.done(V.tensor_tensor_scan(row(2), row(0), row(0), 0.0, amax, amax))
                steps.done(V.scalar_tensor_tensor(row(3), row(1), -1.0, row(2), mult, sub))
                V.tensor_scalar(row(2), row(2), -1.0, None, mult).then_inc(m_row, 1)

            for u in range(8):
                if u < 6:
                    split("cmp", 0, 4, u + 2)
                if u == 2:
                    gate_rows_1()
                if u == 4:
                    gate_rows_2()
                if u == 3 or u == 7:
                    dve.wait_ge(w_used, U0["cmp"] + u + 1)
                    hidden_bias(u // 4)
            dve.wait_ge(cmp_proj, 1)
            V.tensor_copy(kc[:, 0:NCMP], bank[4][:, 0:NCMP]).then_inc(cmp_out, 1)
            V.tensor_copy(vc[0:NCMP, :], bank[5][0:NCMP, 0:P]).then_inc(cmp_out, 1)
            for u in (6, 7, 8, 9):
                split("cmp", 0, 4, u + 2)

            dve.wait_ge(toep_in, 16)
            items, NI = NSA_ITEMS, len(NSA_ITEMS)
            def nsa_lo(c):
                dve.wait_ge(op_hi, R0["nsa"] + c + 1)
                V.tensor_tensor(cut(h_lo, c), bank[4][:], cut(h_hi, c).bitcast(f32), sub).then_inc(op_lo, 1)

            for c in steps.loop(4, 4 + NI, peel=1):
                V.tensor_copy(q_st[:], cut(qT, c)).then_inc(n_q, 1)
                last = None
                for half in range(2):
                    steps.done(V.tensor_copy(backwards(half), cut(toep, c + 4 * half)))
                    src = gate[:].rearrange("p (q h n) -> p q h n", h=2, n=12)[:, :, half, bass.ds(3 * c, 3)]
                    steps.done(V.tensor_copy(gate_st[:, half * 12:(half + 1) * 12].rearrange("p (q r) -> p q r", r=3), src))
                if not isinstance(c, int):
                    nsa_lo(c - 1)
                for s in range(NI + 1):
                    if s < NI:
                        half, qb, br = items[s]
                        n = (8 * qb + 7) if br == 0 else P * (qb + 1)
                        dve.wait_ge(n_qk, NI * c + s + 1)
                        if s >= 2:
                            dve.wait_ge(n_exp, NI * c + s - 1)
                        dve.sem_inc(n_seen, 1)
                        at = half * S
                        bias = (toep_st[:, at + 31 + P * (3 - qb):at + S:16] if br == 0 else toep_st[:, at + S - n:at + S])
                        V.tensor_tensor_reduce(s_sb[:, (s % 2) * S:(s % 2) * S + n], bank[s % 2][:, 0:n], bias, -1.0, 3.0e38,
                                               add, amin, small[:, 8 + s % 2:9 + s % 2]).then_inc(n_add, 1)
                    r = s - 1
                    if r >= 0:
                        half, qb, br = items[r]
                        n = (8 * qb + 7) if br == 0 else P * (qb + 1)
                        dve.wait_ge(n_exp, NI * c + r + 1)
                        inv = small[:, 16 + r % 2:17 + r % 2]
                        steps.done(V.reciprocal(inv, small[:, 12 + r % 2:13 + r % 2]))
                        pr = p_sb[:, (r % 3) * S:(r % 3) * S + n]
                        g = half * 12 + qb * 3 + br
                        V.tensor_scalar(pr, pr, inv, gate_st[:, g:g + 1], mult, mult).then_inc(n_scaled, 1)
            nsa_lo(3)

            dve.wait_ge(m_col, 1)
            V.tensor_copy(a_col[:], bank[2][:, 0:16]).then_inc(m_colout, 1)
            dve.wait_ge(m_colout, 1)

            def ml_finish(hd):
                dve.wait_ge(m_pv, 4 * hd + 4)
                dve.wait_ge(m_floor, hd + 1)
                steps.done(V.scalar_tensor_tensor(t0[:], bank[6 + hd % 2][:], -1.0, floor[:], mult, amax))
                steps.done(V.tensor_tensor(t0[:], bank[6 + hd % 2][:], t0[:], amax))
                steps.done(V.reciprocal(t0[:], t0[:]))
                V.tensor_tensor(cut(h_ml, hd), bank[4 + hd % 2][:], t0[:], mult).then_inc(m_h, 1)

            for i in range(16):
                hd, kb = divmod(i, TB)
                dve.wait_ge(m_bc, hd + 1)
                if i >= 2:
                    dve.wait_ge(m_decay, i - 1)
                V.scalar_tensor_tensor(diag[:, (i % 2) * P:(i % 2 + 1) * P], bank[0][:, kb * P:(kb + 1) * P],
                                       a_col[:, 4 * kb + hd:4 * kb + hd + 1], const("not_after"), add, add).then_inc(m_diag, 1)
                n = S - kb * P
                dve.wait_ge(m_qk, i + 1)
                dve.wait_ge(m_decay, i + 1)
                if i >= 2:
                    dve.wait_ge(m_pv, i - 1)
                V.scalar_tensor_tensor(weight[:, (i % 2) * S:(i % 2) * S + n], bank[2 + i % 2][:, 0:n], DH ** -0.5,
                                       decay[:, (i % 2) * S:(i % 2) * S + n], mult, mult).then_inc(m_weight, 1)
                if kb == 1 and hd:
                    ml_finish(hd - 1)
            ml_finish(3)
            dve.wait_ge(m_root, 1)
            V.reciprocal(rows[0:4, 4 * S:5 * S], rows[0:4, 4 * S:5 * S]).then_inc(m_inv, 1)
            dve.wait_ge(acted_mix, 8)
            for hd in range(4):
                dve.wait_ge(m_factor, hd + 1)
                steps.done(V.scalar_tensor_tensor(cut(h_ml, hd), cut(h_ml, hd), col("mlstm_norm", hd), bank[FACTOR_BANK[hd]][:], mult, mult))
                V.tensor_tensor(cut(h_ml, hd), cut(h_ml, hd), cut(mo, hd), mult).then_inc(m_out, 1)
                dve.wait_ge(op_hi, R0["ml"] + hd + 1)
                V.tensor_tensor(cut(h_lo, 4 + hd), cut(h_ml, hd), cut(h_hi, 4 + hd).bitcast(f32), sub).then_inc(op_lo, 1)
            dve.wait_ge(mem_in, 16)
            for c in range(KC):
                lo_part("mem", c, "mem_norm", mem, m_hi, m_lo, MEM)

            for u in range(8):
                if u >= 2:
                    split("out", 0, 4, u + 2)
                if u == 1:
                    factor("mem", rM, MEM).then_inc(r_done, 1)
                dve.wait_ge(w_used, U0["out"] + u + 1)
                V.tensor_copy(cut(yb_x, u), bank[u % 4][:]).then_inc(evacuated, 1)
            split("xkv", 0, 4, 2)
            steps.done(factor("post_mix"))
            dve.wait_ge(r_done, 1)
            for u in range(8):
                if u:
                    split("xkv", 0, 4, u + 2)
                post_chunk(u, yb_x, "mix_norm_post")
                dve.wait_ge(w_used, U0["xkv"] + u + 1)
                scaled(cut(kx, u, MEM), bank[u % 4][:, 0:MEM], rM[:]).then_inc(evacuated, 1)
                if u >= 2:
                    lo_part("xq", u - 2, "xattn_norm_pre")
            for c in (KC - 2, KC - 1):
                lo_part("xq", c, "xattn_norm_pre")
            vx3 = vx[:].rearrange("p (b f) -> p b f", f=D)
            for it in rounds(dve, 2):
                for j in range(4):
                    split("xkv", it + 2, 4, j + 2)
                    dve.wait_ge(w_used, U0["xkv"] + 8 + 4 * it + j + 1)
                    i = 6 + 4 * it + j
                    if j >= 2:
                        dve.wait_ge(v_turned, i - 1)
                    scaled((t0, t1)[j % 2][:, 0:MEM], bank[j][:, 0:MEM], rM[:]).then_inc(evacuated, 1)
                    dve.wait_ge(evacuated, B0["xkv"] + 8 + 4 * it + j + 1)
                    dve.sem_inc(v_ready, 1)
                    if j:
                        turn_in(i - 1, (j - 1) % 2, vx3[:, :, bass.ds((4 * it + j - 1) * P, P)], MEM)
                turn_in(6 + 4 * it + 3, 1, vx3[:, :, bass.ds((4 * it + 3) * P, P)], MEM)

            def xq_out(it, j):
                scaled(cut(qx, 4 * it + j), bank[j][:], by=256 ** -0.5).then_inc(evacuated, 1)
            stage("xq", "xq", xq_out)
            for s in range(16 + 1):
                if s < 16:
                    dve.wait_ge(x_qk, s + 1)
                    V.tensor_reduce(small[:, 8 + s % 2:9 + s % 2], bank[s % 2][:, 0:MEM], AX.X, amax, negate=True).then_inc(x_max, 1)
                r = s - 1
                if r >= 0:
                    dve.wait_ge(x_exp, r + 1)
                    inv = small[:, 16 + r % 2:17 + r % 2]
                    steps.done(V.reciprocal(inv, small[:, 12 + r % 2:13 + r % 2]))
                    V.tensor_scalar(cut(px, r % 3, MEM), cut(px, r % 3, MEM), inv, None, mult).then_inc(x_scaled, 1)
                if s >= 6 and s % 4 == 2 or s == 16:
                    heads = [(s - 6) // 4] if s < 16 else [3]
                    for hd in heads:
                        for dv in range(2):
                            c = 2 * hd + dv
                            dve.wait_ge(op_hi, R0["xo"] + c + 1)
                            V.tensor_tensor(cut(h_lo, c), bank[4 + dv][:], cut(h_hi, c).bitcast(f32), sub).then_inc(op_lo, 1)

            def xo_out(it, j):
                V.tensor_copy(cut(yb_x, 4 * it + j), bank[j][:]).then_inc(evacuated, 1)
            stage("xo", None, xo_out)
            post("post_x", yb_x, "xattn_norm_post", "gu0", "ffn_norm_pre")
            gate_up("gu0", 0, "gu0")

            def dn0_out(it, j):
                if j % 3 == 2:
                    V.tensor_copy(cut(yb_h, 4 * it + j // 3), bank[j // 3][:]).then_inc(evacuated, 1)
            stage("dn0", None, dn0_out, per=12)
            post("post_ffn", yb_h, "ffn_norm_post", "gu1", "ffn1_0")
            gate_up("gu1", 1, "gu1")
            down("dn1", "pw1", "mix_0")
            V.memset(u_conv[:].rearrange("p (c n) -> p c n", n=S + PAD)[:, :, 0:PAD], 0.0).then_inc(pad_done, 1)

            def taps(pair, i0, i1):
                for i in range(i0, i1):
                    for s in range(2):
                        c = 2 * pair + s
                        cv_c = cut(cv, c)
                        k = TAPS - TAPS_DVE + i
                        if i == 0:
                            dve.wait_ge(c_glu, c + 1)
                        else:
                            dve.wait_ge(c_taps, taps_done(pair, i - 1, s))
                        if i == TAPS_DVE:
                            dve.wait_ge(c_pe, c + 1)
                            done = V.tensor_tensor(cv_c, cv_c, bank[4 + s][:], add)
                        else:
                            u, w = u_conv[:, bass.ds(c * (S + PAD) + k, S)], col("w_dw", c * TAPS + k)
                            if i == 0:
                                done = V.tensor_scalar(cv_c, u, w, None, mult)
                            else:
                                done = V.scalar_tensor_tensor(cv_c, u, w, cv_c, mult, add)
                        done.then_inc(c_taps, 1)

            quarters = [(TAPS_DVE + 1) * j // 4 for j in range(5)]
            split("pw1", 0, 4, 2)
            steps.done(factor("pw1"))
            dve.wait_ge(pad_done, 3)
            for it in rounds(dve, KC // 2, peel=1):
                first = isinstance(it, int) and it == 0
                for j in range(4):
                    if not (first and j == 0):
                        split("pw1", it, 4, j + 2)
                    if not first:
                        taps(it - 1, quarters[j], quarters[j + 1])
                    if j == 2 or j == 0 and not first:
                        dve.wait_ge(c_glu, 2 * it + j // 2)
                    dve.wait_ge(w_used, U0["pw1"] + 4 * it + j + 1)
                    scaled((t1, t0)[j % 2][:], bank[j][:]).then_inc(evacuated, 1)
                    if j % 2:
                        c = 2 * it + j // 2
                        dve.wait_ge(acted, ACTED0["pw1"] + c + 1)
                        V.scalar_tensor_tensor(u_conv[:, bass.ds(c * (S + PAD) + PAD, S)], t1[:], col("b_pw1", c), t0[:],
                                               add, mult).then_inc(c_glu, 1)
            taps(KC // 2 - 1, 0, TAPS_DVE + 1)
            dve.wait_ge(root_done, NORM["ln_mean"] + 1)
            dve.wait_ge(c_conv, KC)
            for c in range(KC):
                V.tensor_tensor(cut(cv, c), cut(cv, c), rB[:], sub).then_inc(c_cent, 1)
            steps.done(factor("ln_var"))
            for c in range(KC + 1):
                if c < KC:
                    V.tensor_tensor(cut(cv, c), cut(cv, c), rB[:], mult).then_inc(c_norm, 1)
                if c:
                    lo_part("pw2", c - 1, None, cv, o_hi, o_lo)

            def result(name, operand, gain, bias):
                def after(it, j):
                    c = 4 * it + j
                    V.scalar_tensor_tensor(cut(x, c), bank[j][:], 0.0 if bias is None else col(bias, c), cut(x, c), add, add).then_inc(evacuated, 1)
                    lo_part(operand, c, gain)
                stage(name, None, after)

            result("pw2", "gu2", "ffn2_0", "b_pw2")
            gate_up("gu2", 2, "gu2")
            down("dn2", "kv", "kv_norm")

            def spill(n0, per_round, by=None):
                def after(it, j):
                    n = n0 + per_round * it + j
                    if not (isinstance(it, int) and n < 2):
                        dve.wait_ge(spilled[j % 2], 8 * (n - j % 2))
                    scaled((t0, t1)[j % 2][:], bank[j][:], by=by).then_inc(evacuated, 1)
                return after
            stage("kv", "kv", spill(0, 4))
            for c in range(KC):
                lo_part("gu3", c, "ffn1_1")
            for par in range(2):
                dve.wait_ge(spilled[par], 16 * 8)
            gate_up("gu3", 3, None)
            down("dn3", "q", "mix_1")
            stage("q", "q", spill(16, 4, DH ** -0.5))

            V.tensor_copy(ident_b[:], ident).then_inc(s_const, 1)
            V.tensor_copy(mask_b[:], const("mask_from_query")).then_inc(s_const, 1)

            def stick_out(p):
                dve.wait_ge(op_hi, R0["o"] + p + 1)
                V.tensor_tensor(cut(o_lo, p), bank[3][:], cut(o_hi, p).bitcast(f32), sub).then_inc(op_lo, 1)

            for it in rounds(dve, KC // 2, peel=1):
                first = isinstance(it, int) and it == 0
                for jj in range(4):
                    g = 4 * it + jj
                    z, e = banks[jj % 2][:, 0:STICK], s_l[:, jj % 2 * STICK:(jj % 2 + 1) * STICK]
                    dve.wait_ge(s_qk, g + 1)
                    if not (first and jj < 2):
                        dve.wait_ge(s_sum, g - 1)
                    V.tensor_scalar(e, z, 40.0, None, amin).then_inc(s_clip, 1)
                    dve.wait_ge(s_log, g + 1)
                    V.tensor_tensor(e, z, e, amax).then_inc(s_soft, 1)
                    dve.wait_ge(s_soft, g + 1)
                    l1, l2, l3 = (e[:, STICKS[kb][0]:STICKS[kb][0] + STICKS[kb][1]] for kb in (1, 2, 3))
                    later = [s_later[:, (jj % 2 * 3 + m) * P:(jj % 2 * 3 + m + 1) * P] for m in range(3)]
                    V.tensor_tensor(later[0], l2[:, P:2 * P], l3, add).then_inc(s_added, 1)
                    V.tensor_tensor(later[1], l1[:, P:2 * P], l2[:, 0:P], add).then_inc(s_added, 1)
                    dve.wait_ge(s_added, 3 * g + 1)
                    V.tensor_tensor(later[2], l1[:, 2 * P:3 * P], later[0], add).then_inc(s_added, 1)
                    if jj % 2 and not (first and jj == 1):
                        stick_out(2 * it + jj // 2 - 1)
            stick_out(KC - 1)
            result("o", "gu4", "ffn2_1", None)
            gate_up("gu4", 4, "gu4")
            down("dn4", "final", None)
            steps.done(factor("final"))
            for c in range(KC):
                V.scalar_tensor_tensor(cut(x, c), cut(x, c), col("final_norm", c), rB[:], mult, mult).then_inc(last_out, 1)

        @block.gpsimd
        def _(pool):
            G = nc.gpsimd
            pool.dma_start(onehot[0:32, 0:S + 8], t["onehot_rel"]).then_inc(rel_in, 16)
            pool.dma_start(cmp_w2[:], t["cmp_w2"]).then_inc(w2_in, 16)
            pool.dma_start(gbias[0:4, :], t["gate_bias"]).then_inc(gb_in, 16)

            def sum_chunks(name, n=S):
                base = SUM0[name]
                if NORM[name]:
                    pool.wait_ge(stat_done, NORM[name])
                G.memset(acc[:, 0:n], 0.0).then_inc(summed, 1)
                for c in range(KC):
                    pool.wait_ge(squared, SQ0[name] + c + 1)
                    pool.wait_ge(summed, base + c + 1)
                    G.tensor_tensor(acc[:, 0:n], acc[:, 0:n], sq[:, (c % 2) * S:(c % 2) * S + n], add).then_inc(summed, 1)

            sum_chunks("mix")
            pool.wait_ge(bias_sb, 1)
            pool.wait_ge(bias_fill, 1)
            pool.dma_start(bias_dram, r_bias[0:8, :]).then_inc(bias_out, 16)
            pool.wait_ge(bias_out, 16)
            pool.dma_start(toep[:].rearrange("p (h n) -> p h n", n=S),
                           bass.AP(tensor=bias_dram.tensor, offset=1, ap=[[1, P], [HBM_BIAS, 8], [1, S]])).then_inc(toep_in, 16)
            pool.wait_ge(op_lo, R0["ml"] + 4)
            pool.dma_start(mem[:], t["mem"].rearrange("p c n -> p (c n)")).then_inc(mem_in, 16)
            sum_chunks("mem", MEM)
            sum_chunks("post_mix")
            sum_chunks("xq")
            sum_chunks("post_x")
            sum_chunks("gu0")
            sum_chunks("post_ffn")
            sum_chunks("gu1")
            sum_chunks("pw1")
            for pair in range(KC // 2):
                for c in (2 * pair, 2 * pair + 1):
                    acc_c = cut(c_acc, c % 2)
                    for i in range(1, TAPS_POOL):
                        n = c * TAPS_POOL + i
                        if i > 1:
                            pool.wait_ge(c_product_used, n)
                        elif pair:
                            pool.wait_ge(c_conv, c - 1)
                        pool.wait_ge(c_product_made, n + 1)
                        G.tensor_tensor(acc_c, cut(c_product, (n - 1) % 2) if i == 1 else acc_c, cut(c_product, n % 2),
                                        add).then_inc(c_product_used, 2 if i == 1 else 1)
                for c in (2 * pair, 2 * pair + 1):
                    pool.wait_ge(c_taps, taps_done(pair, TAPS_DVE, c % 2))
                    pool.wait_ge(c_product_used, (c + 1) * TAPS_POOL)
                    G.tensor_tensor(cut(cv, c), cut(cv, c), cut(c_acc, c % 2), add).then_inc(c_conv, 1)
            sum_chunks("ln_var")
            sum_chunks("gu2")
            sum_chunks("kv")
            sum_chunks("q")
            sum_chunks("gu4")
            sum_chunks("final")


_VECTORS = {
    "mix_norm_pre": "mix_norm_pre", "mix_norm_post": "mix_norm_post", "xattn_norm_pre": "xattn_norm_pre",
    "mem_norm": "mem_norm", "xattn_norm_post": "xattn_norm_post", "ffn_norm_pre": "ffn_norm_pre",
    "ffn_norm_post": "ffn_norm_post", "kv_norm": "kv_norm_2", "final_norm": "final_norm_2", "b_dw": "conv_b_dw_2",
    "ln_g": "conv_ln_g_2", "ln_b": "conv_ln_b_2", "b_pw2": "conv_b_pw2_2", "conv_b": "conv_b", "mlstm_norm": "mlstm_norm",
}


def columns(v):
    return v.reshape(-1, P).T


def weight_blocks(w):
    k, n = w.shape
    return np.ascontiguousarray(w.reshape(k // P, P, n // P, P).transpose(2, 1, 0, 3))


def interleave(a, b):
    k, n = a.shape
    return np.stack([a.reshape(k, n // P, P), b.reshape(k, n // P, P)], axis=2).reshape(k, 2 * n)


def buckets_by_distance():
    n = np.arange(S)
    exact = 16
    large = exact + (np.log(np.maximum(n, 1).astype(np.float32) / np.float32(exact))
                     / np.float32(np.log(128 / exact)) * np.float32(32 - exact)).astype(np.int32)
    bucket = np.where(n < exact, n, np.minimum(large, 31))
    return (np.arange(32)[:, None] == bucket[None, :]).astype(np.float32)


def constants():
    r = np.arange(P)
    one = np.ones((P, P), np.float32)
    made = {
        "ident": np.eye(P, dtype=np.float32), "ones": one, "minus_ones": -one,
        "mask_from_query": (r[None, :] >= r[:, None]) * np.float32(-1e30),
        "minus_from_here": -(r[:, None] >= r[None, :]).astype(np.float32),
        "not_after": np.where(r[:, None] > r[None, :], np.float32(NEG), np.float32(0)),
        "to_row": np.repeat(np.eye(4, dtype=np.float32).reshape(1, 16), P, axis=0),
        "pick": np.repeat((r[:, None] == np.arange(4)[None, :]).astype(np.float32), P, axis=1),
        "has_block": (r[:, None] >= 31).astype(np.float32), "one": one[:, :1], "zero": 0 * one[:, :1],
        "norm_eps": one[:, :1] * np.float32(1e-6), "ln_eps": one[:, :1] * np.float32(1e-5),
    }
    return np.ascontiguousarray(np.concatenate([made[n] for n, _ in CONSTS], axis=1), dtype=np.float32)


def lay_out(a):
    vec = {n: columns(a[src].reshape(-1)) for n, src in _VECTORS.items()}
    for i in range(2):
        vec[f"ffn1_{i}"], vec[f"mix_{i}"] = columns(a["ffn1_norm_2"][i]), columns(a["mix_norm_2"][i])
        vec[f"ffn2_{i}"] = columns(a["ffn2_norm_2"][i])
    vec["b_pw1"] = columns(a["conv_b_pw1_2"][0])
    vec["w_dw"] = a["conv_w_dw_2"][0].reshape(TAPS, KC, P).transpose(2, 1, 0).reshape(P, -1)
    vec["conv_w"] = a["conv_w"][0].reshape(4, 4, P).transpose(2, 1, 0).reshape(P, -1)
    for n in "kv":
        vec[f"pos_{n}"] = a[f"cmp_pos_{n}"][0].reshape(16, P).T
    w = a["w_in"][0]
    parts = np.split(w, np.cumsum([512] + [128] * 6 + [24, 256, 256, 512, 4, 4]), axis=1)
    nq, kc, vc, ks, vs, kw, vw, gt, mq, mk, mv, mi, mf, mo = parts
    heads = [h for c in range(4) for h in (c, c + 4)]
    nq = nq.reshape(D, 8, DH)[:, heads].reshape(D, 512)
    w_in = np.concatenate([nq, kc, vc, ks, kw, vs, vw, mv, mq, mk, mo], axis=1)
    gates = np.zeros((D, P), np.float32)
    gates[:, GT:GT + 24], gates[:, MI:MI + 4], gates[:, MF:MF + 4] = gt, mi, mf
    w_out = a["w_out"][0]
    w_out = np.concatenate([w_out[:512].reshape(8, DH, D)[heads].reshape(512, D), w_out[512:]], axis=0)
    half = lambda m: np.split(m, 2, axis=1)
    laid = {
        "vectors": np.ascontiguousarray(np.concatenate([vec[n] for n, _ in VECTORS], axis=1)),
        "consts": constants(),
        "x": np.ascontiguousarray(a["x"][0].T.reshape(KC, P, S).transpose(1, 0, 2)),
        "mem": np.ascontiguousarray(a["mem"][0].T.reshape(KC, P, MEM).transpose(1, 0, 2)),
        "onehot_rel": np.ascontiguousarray(np.concatenate([buckets_by_distance(), a["rel_bias"].T], axis=1)),
        "cmp_w2": np.ascontiguousarray(np.stack([a["cmp_w2_k"][0].reshape(2, P, DH), a["cmp_w2_v"][0].reshape(2, P, DH)])
                                       .transpose(2, 0, 1, 3).reshape(P, -1)),
        "gate_bias": np.ascontiguousarray(a["mlstm_gate_bias"][0].T),
        "w_in": weight_blocks(w_in), "w_gates": weight_blocks(gates)[0],
        "cmp_w1": np.ascontiguousarray(np.concatenate([a["cmp_w1_k"][0], a["cmp_w1_v"][0]])
                                       .reshape(8, 4, P, 2 * P).transpose(0, 2, 1, 3)),
        "w_out": weight_blocks(w_out), "w_xkv": weight_blocks(a["w_xkv"][0]), "w_xq": weight_blocks(a["w_xq"][0]),
        "w_xo": weight_blocks(a["w_xo"][0]),
        "w_gu0": weight_blocks(interleave(*half(a["w_gate_up"][0]))), "w_dn0": weight_blocks(a["w_down"][0]),
        "w_pw1": weight_blocks(interleave(*half(a["conv_w_pw1_2"][0]))), "w_pw2": weight_blocks(a["conv_w_pw2_2"][0]),
        "w_kv": weight_blocks(a["w_kv_2"]), "w_q": weight_blocks(a["attn_w_q_2"][0]), "w_o": weight_blocks(a["attn_w_o_2"][0]),
    }
    for n, (ffn, layer) in enumerate([("ffn1", 0), ("ffn2", 0), ("ffn1", 1), ("ffn2", 1)], start=1):
        laid[f"w_gu{n}"] = weight_blocks(interleave(a[f"{ffn}_w_gate_2"][layer], a[f"{ffn}_w_up_2"][layer]))
        laid[f"w_dn{n}"] = weight_blocks(a[f"{ffn}_w_down_2"][layer])
    return laid


def kernel(**inputs):
    import concourse.bacc as bacc
    from concourse.bass_utils import run_bass_kernel_spmd as run

    nc = bacc.Bacc("TRN2", target_bir_lowering=False, num_devices=1)
    laid = lay_out({n: np.asarray(v) for n, v in inputs.items()})
    t = {n: nc.dram_tensor("in_" + n, v.shape, mybir.dt.from_np(v.dtype), kind="ExternalInput").ap() for n, v in laid.items()}
    out = nc.dram_tensor("out", (P, KC * S), mybir.dt.float32, kind="ExternalOutput").ap()
    block_program(nc, t, out)
    got = run(nc, [{"in_" + n: v for n, v in laid.items()}], core_ids=[0]).results[0]["out"]
    return np.ascontiguousarray(got.reshape(P, KC, S).transpose(2, 1, 0).reshape(1, S, D))
```
